# Optimizing a Trainium2 kernel written in Bass

```python
import math
import jax, jax.numpy as jnp
from jax import lax
import numpy as np

D_MODEL = 1024
BATCH = 1
SEQ = 256
DEPTH = 1
DEC_BATCH = 8
DEC_SEQ = 4
PAST_LEN = 1024
PAGE_SIZE = 128

SSD_HEADS = 16
SSD_HEAD_DIM = 64
SSD_INNER = SSD_HEADS * SSD_HEAD_DIM
SSD_GROUPS = 2
SSD_STATE = 128
SSD_CONV = 4
SSD_CHUNK = 128
CONV_DIM = SSD_INNER + 2 * SSD_GROUPS * SSD_STATE
ATT_HEADS = 8
ATT_HEAD_DIM = 64
ATT_WIDTH = ATT_HEADS * ATT_HEAD_DIM
DILATED_PATTERNS = ((128, 1), (512, 4), (2048, 16))
MAX_WINDOW = 2048
ATT_BLOCK = 128
MIX_WIDTH = SSD_INNER + ATT_WIDTH
IN_WIDTH = SSD_INNER + CONV_DIM + SSD_HEADS + 3 * ATT_WIDTH
N_EXPERTS = 32
TOP_K = 4
D_EXPERT = D_MODEL
SWIGLU_LIMIT = 7.0
SWIGLU_ALPHA = 1.702
MOE_BLOCK = 128
NORM_EPS = 1e-5

kernel_name = 'hymba_ssd_dilated_swa_moe_step'

def rmsnorm(x, g):
    xf = x.astype(jnp.float32)
    y = xf * lax.rsqrt(jnp.mean(xf * xf, axis=-1, keepdims=True) + NORM_EPS)
    return (y * g.astype(jnp.float32)).astype(x.dtype)

def alibi_slopes():
    return jnp.exp2(-8.0 * jnp.arange(1, ATT_HEADS + 1, dtype=jnp.float32) / ATT_HEADS)

def split_in(u):
    o = 0
    parts = []
    for w in (SSD_INNER, CONV_DIM, SSD_HEADS, ATT_WIDTH, ATT_WIDTH, ATT_WIDTH):
        parts.append(u[..., o:o + w])
        o += w
    return parts

def causal_dwconv(xp, w, b):
    L = xp.shape[1] - (SSD_CONV - 1)
    out = b
    for j in range(SSD_CONV):
        out = out + xp[:, j:j + L] * w[j]
    return out

def segsum(a):
    T = a.shape[-1]
    ab = jnp.broadcast_to(a[..., :, None], a.shape + (T,))
    strict = jnp.tril(jnp.ones((T, T), bool), -1)
    cs = jnp.cumsum(jnp.where(strict, ab, 0.0), axis=-2)
    return jnp.where(jnp.tril(jnp.ones((T, T), bool)), cs, -jnp.inf)

def ssd_chunked(xh, dt, A, Bg, Cg, init_state, chunk):
    b, L, H, P = xh.shape
    G, N = Bg.shape[2], Bg.shape[3]
    E = H // G
    c = L // chunk
    X = (xh * dt[..., None]).reshape(b, c, chunk, G, E, P)
    dA = (dt * A).reshape(b, c, chunk, G, E).transpose(0, 1, 3, 4, 2)
    Bc = Bg.reshape(b, c, chunk, G, N)
    Cc = Cg.reshape(b, c, chunk, G, N)
    cs = jnp.cumsum(dA, axis=-1)
    Lmat = jnp.exp(segsum(dA))
    CB = jnp.einsum('bclgn,bcsgn->bcgls', Cc, Bc)
    y_diag = jnp.einsum('bcgels,bcsgep->bclgep', CB[:, :, :, None] * Lmat, X)
    decay_states = jnp.exp(cs[..., -1:] - cs).transpose(0, 1, 4, 2, 3)
    states = jnp.einsum('bclgn,bclgep->bcgepn', Bc, X * decay_states[..., None])
    states = jnp.concatenate([init_state.reshape(b, G, E, P, N)[:, None], states], axis=1)
    tot = jnp.pad(cs[..., -1].transpose(0, 2, 3, 1), ((0, 0), (0, 0), (0, 0), (1, 0)))
    decay_chunk = jnp.exp(segsum(tot))
    new_states = jnp.einsum('bgezc,bcgepn->bzgepn', decay_chunk, states)
    prev_states, final = new_states[:, :-1], new_states[:, -1]
    y_off = jnp.einsum('bclgn,bcgepn->bclgep', Cc, prev_states) * jnp.exp(cs).transpose(0, 1, 4, 2, 3)[..., None]
    y = (y_diag + y_off).reshape(b, L, H, P)
    return y, final.reshape(b, H, P, N)

def ssd_branch(z, xbc_act, dt_raw, init_state, dt_bias, a_log, d_skip, ssd_norm):
    b, L, _ = xbc_act.shape
    f32 = jnp.float32
    gn = SSD_GROUPS * SSD_STATE
    xh = xbc_act[..., :SSD_INNER].reshape(b, L, SSD_HEADS, SSD_HEAD_DIM).astype(f32)
    Bg = xbc_act[..., SSD_INNER:SSD_INNER + gn].reshape(b, L, SSD_GROUPS, SSD_STATE).astype(f32)
    Cg = xbc_act[..., SSD_INNER + gn:].reshape(b, L, SSD_GROUPS, SSD_STATE).astype(f32)
    dt = jax.nn.softplus(dt_raw.astype(f32) + dt_bias.astype(f32))
    A = -jnp.exp(a_log.astype(f32))
    chunk = SSD_CHUNK if L % SSD_CHUNK == 0 else L
    y, final = ssd_chunked(xh, dt, A, Bg, Cg, init_state.astype(f32), chunk)
    y = y + d_skip.astype(f32)[:, None] * xh
    y = y.reshape(b, L, SSD_INNER) * jax.nn.silu(z.astype(f32))
    yg = y.reshape(b, L, SSD_GROUPS, SSD_INNER // SSD_GROUPS)
    yg = yg * lax.rsqrt(jnp.mean(yg * yg, axis=-1, keepdims=True) + NORM_EPS)
    return yg.reshape(b, L, SSD_INNER) * ssd_norm.astype(f32), final

def merge_by_denominator(outs, lses):
    w = jax.nn.softmax(jnp.stack(lses, 0), axis=0)
    return jnp.einsum('pblh,pblhe->blhe', w, jnp.stack(outs, 0))

def dilated_attn_prompt(q, k, v, slopes):
    b, S, H, e = q.shape
    scale = ATT_HEAD_DIM ** -0.5
    outs, lses = [], []
    for window, dil in DILATED_PATTERNS:
        span = window // dil
        sc = S // dil
        nb = -(-sc // ATT_BLOCK)
        pad = nb * ATT_BLOCK - sc

        def to_blocks(t):
            t = t.reshape(b, sc, dil, H, e).transpose(0, 2, 1, 3, 4)
            t = jnp.pad(t, ((0, 0), (0, 0), (0, pad), (0, 0), (0, 0)))
            return t.reshape(b, dil, nb, ATT_BLOCK, H, e)

        def with_prev(t):
            prev = jnp.pad(t[:, :, :-1], ((0, 0), (0, 0), (1, 0), (0, 0), (0, 0), (0, 0)))
            return jnp.concatenate([prev, t], axis=3)

        qb = to_blocks(q)
        kk = with_prev(to_blocks(k))
        vv = with_prev(to_blocks(v))
        s = jnp.einsum('brnqhe,brnkhe->brnhqk', qb, kk) * scale
        qi = jnp.arange(ATT_BLOCK)[:, None] + ATT_BLOCK
        kj = jnp.arange(2 * ATT_BLOCK)[None, :]
        delta = qi - kj
        blk = jnp.arange(nb)[:, None, None]
        valid = (delta >= 0) & (delta <= span) & (blk * ATT_BLOCK + kj - ATT_BLOCK >= 0)
        bias = -slopes[:, None, None] * (dil * delta).astype(jnp.float32)[None]
        s = jnp.where(valid[:, None], s + bias, -jnp.inf)
        lse = jax.nn.logsumexp(s, axis=-1)
        o = jnp.einsum('brnhqk,brnkhe->brnqhe', jnp.exp(s - lse[..., None]), vv)
        o = o.reshape(b, dil, nb * ATT_BLOCK, H, e)[:, :, :sc].transpose(0, 2, 1, 3, 4).reshape(b, S, H, e)
        lse = lse.transpose(0, 1, 2, 4, 3).reshape(b, dil, nb * ATT_BLOCK, H)[:, :, :sc]
        lse = lse.transpose(0, 2, 1, 3).reshape(b, S, H)
        outs.append(o)
        lses.append(lse)
    return merge_by_denominator(outs, lses)

def dilated_attn_decode(q, k_all, v_all, slopes):
    T = q.shape[1]
    M = k_all.shape[1] - T
    scale = ATT_HEAD_DIM ** -0.5
    outs, lses = [], []
    for window, dil in DILATED_PATTERNS:
        steps = jnp.arange(window // dil + 1)
        idx = M + jnp.arange(T)[:, None] - dil * steps[None, :]
        valid = idx >= 0
        idx_c = jnp.maximum(idx, 0)
        kg = k_all[:, idx_c]
        vg = v_all[:, idx_c]
        s = jnp.einsum('bthe,btkhe->bthk', q, kg) * scale
        bias = -slopes[:, None] * (dil * steps).astype(jnp.float32)[None, :]
        s = jnp.where(valid[:, None, :], s + bias, -jnp.inf)
        lse = jax.nn.logsumexp(s, axis=-1)
        outs.append(jnp.einsum('bthk,btkhe->bthe', jnp.exp(s - lse[..., None]), vg))
        lses.append(lse)
    return merge_by_denominator(outs, lses)

def token_mixer(hn, conv_prev, ssm_prev, win_k_prev, win_v_prev, slopes,
                w_in, conv_w, conv_b, dt_bias, a_log, d_skip, ssd_norm, att_norm, w_out):
    b, L, _ = hn.shape
    f32 = jnp.float32
    z, xbc, dt_raw, q, k, v = split_in(hn @ w_in)
    xbc_ext = jnp.concatenate([conv_prev.astype(xbc.dtype), xbc], axis=1)
    new_conv = xbc_ext[:, -(SSD_CONV - 1):]
    xbc_act = jax.nn.silu(causal_dwconv(xbc_ext, conv_w, conv_b))
    y_ssd, new_ssm = ssd_branch(z, xbc_act, dt_raw, ssm_prev, dt_bias, a_log, d_skip, ssd_norm)
    q = q.reshape(b, L, ATT_HEADS, ATT_HEAD_DIM).astype(f32)
    k = k.reshape(b, L, ATT_HEADS, ATT_HEAD_DIM).astype(f32)
    v = v.reshape(b, L, ATT_HEADS, ATT_HEAD_DIM).astype(f32)
    if win_k_prev is None:
        o = dilated_attn_prompt(q, k, v, slopes)
        keep = min(MAX_WINDOW, L)
        new_k, new_v = k[:, L - keep:], v[:, L - keep:]
    else:
        k_all = jnp.concatenate([win_k_prev.astype(f32), k], axis=1)
        v_all = jnp.concatenate([win_v_prev.astype(f32), v], axis=1)
        o = dilated_attn_decode(q, k_all, v_all, slopes)
        new_k, new_v = k, v
    o = rmsnorm(o.reshape(b, L, ATT_WIDTH), att_norm)
    y = jnp.concatenate([y_ssd, o], axis=-1) @ w_out
    return y, new_conv, new_ssm, new_k, new_v

def moe_ffn(xf, router_w, router_b, w1, b1, w2, b2):
    n_tok, d = xf.shape
    logits = (xf @ router_w).astype(jnp.float32) + router_b.astype(jnp.float32)
    top_val, top_idx = lax.top_k(logits, TOP_K)
    gates = jax.nn.softmax(top_val, axis=-1)
    n_asg = n_tok * TOP_K
    e_flat = top_idx.reshape(-1)
    tok_flat = jnp.arange(n_asg, dtype=jnp.int32) // TOP_K
    order = jnp.argsort(e_flat)
    e_sorted = e_flat[order]
    counts = jnp.bincount(e_flat, length=N_EXPERTS)
    padded = (counts + MOE_BLOCK - 1) // MOE_BLOCK * MOE_BLOCK
    pad_end = jnp.cumsum(padded)
    pad_start = pad_end - padded
    start = jnp.cumsum(counts) - counts
    dest = pad_start[e_sorted] + jnp.arange(n_asg, dtype=jnp.int32) - start[e_sorted]
    n_blocks = -(-n_asg // MOE_BLOCK) + N_EXPERTS
    n_slots = n_blocks * MOE_BLOCK
    slot_tok = jnp.full((n_slots,), n_tok, jnp.int32).at[dest].set(tok_flat[order])
    slot_gate = jnp.zeros((n_slots,), jnp.float32).at[dest].set(gates.reshape(-1)[order])
    block_expert = jnp.minimum(
        jnp.searchsorted(pad_end, jnp.arange(n_blocks, dtype=pad_end.dtype) * MOE_BLOCK, side='right'),
        N_EXPERTS - 1)
    x_pad = jnp.concatenate([xf, jnp.zeros((1, d), xf.dtype)], axis=0)
    xs = x_pad[slot_tok].reshape(n_blocks, MOE_BLOCK, d)

    def expert_block(args):
        xb, e = args
        hcat = xb @ w1[e] + b1[e]
        x_glu = jnp.minimum(hcat[:, ::2], SWIGLU_LIMIT)
        x_lin = jnp.clip(hcat[:, 1::2], -SWIGLU_LIMIT, SWIGLU_LIMIT)
        g = x_glu * jax.nn.sigmoid(SWIGLU_ALPHA * x_glu) * (x_lin + 1.0)
        return g @ w2[e] + b2[e]

    ys = lax.map(expert_block, (xs, block_expert))
    ys = ys.reshape(n_slots, d).astype(jnp.float32) * slot_gate[:, None]
    return jnp.zeros((n_tok + 1, d), jnp.float32).at[slot_tok].add(ys)[:n_tok]

def channel_mixer(hn, router_w, router_b, w1, b1, w2, b2):
    b, L, d = hn.shape
    return moe_ffn(hn.reshape(b * L, d), router_w, router_b, w1, b1, w2, b2).reshape(b, L, d)

def setup_inputs(seed: int = 0) -> dict:
    key = jax.random.key(seed)
    ks = jax.random.split(key, 24)
    f32 = jnp.float32
    buf = min(MAX_WINDOW, PAST_LEN)

    def nrm(k, shape, scale):
        return scale * jax.random.normal(k, shape, f32)

    dt0 = jnp.exp(jax.random.uniform(ks[7], (DEPTH, SSD_HEADS), f32, math.log(1e-3), math.log(1e-1)))
    return {
        'x_prompt': nrm(ks[0], (BATCH, SEQ, D_MODEL), 1.0),
        'x_sample': nrm(ks[1], (DEC_BATCH, DEC_SEQ, D_MODEL), 1.0),
        'state_conv': nrm(ks[2], (DEPTH, DEC_BATCH, SSD_CONV - 1, CONV_DIM), 1.0),
        'state_ssm': nrm(ks[3], (DEPTH, DEC_BATCH, SSD_HEADS, SSD_HEAD_DIM, SSD_STATE), 0.5),
        'cache_win_k': nrm(ks[4], (DEPTH, DEC_BATCH, buf, ATT_HEADS, ATT_HEAD_DIM), 1.0),
        'cache_win_v': nrm(ks[5], (DEPTH, DEC_BATCH, buf, ATT_HEADS, ATT_HEAD_DIM), 1.0),
        'norm_mix': 1.0 + nrm(ks[6], (DEPTH, D_MODEL), 0.02),
        'w_in': nrm(ks[8], (DEPTH, D_MODEL, IN_WIDTH), D_MODEL ** -0.5),
        'conv_w': nrm(ks[9], (DEPTH, SSD_CONV, CONV_DIM), SSD_CONV ** -0.5),
        'conv_b': nrm(ks[10], (DEPTH, CONV_DIM), 0.02),
        'dt_bias': dt0 + jnp.log(-jnp.expm1(-dt0)),
        'a_log': jnp.log(jax.random.uniform(ks[11], (DEPTH, SSD_HEADS), f32, 1.0, 16.0)),
        'd_skip': 1.0 + nrm(ks[12], (DEPTH, SSD_HEADS), 0.1),
        'ssd_norm': 1.0 + nrm(ks[13], (DEPTH, SSD_INNER), 0.02),
        'att_norm': 1.0 + nrm(ks[14], (DEPTH, ATT_WIDTH), 0.02),
        'w_out': nrm(ks[15], (DEPTH, MIX_WIDTH, D_MODEL), MIX_WIDTH ** -0.5),
        'norm_ffn': 1.0 + nrm(ks[16], (DEPTH, D_MODEL), 0.02),
        'router_w': nrm(ks[17], (DEPTH, D_MODEL, N_EXPERTS), D_MODEL ** -0.5),
        'router_b': nrm(ks[18], (DEPTH, N_EXPERTS), 0.01),
        'w1': nrm(ks[19], (DEPTH, N_EXPERTS, D_MODEL, 2 * D_EXPERT), D_MODEL ** -0.5),
        'b1': nrm(ks[20], (DEPTH, N_EXPERTS, 2 * D_EXPERT), 0.01),
        'w2': nrm(ks[21], (DEPTH, N_EXPERTS, D_EXPERT, D_MODEL), D_EXPERT ** -0.5),
        'b2': nrm(ks[22], (DEPTH, N_EXPERTS, D_MODEL), 0.01),
        'norm_final': 1.0 + nrm(ks[23], (D_MODEL,), 0.02),
    }

def reference(x_prompt, x_sample, state_conv, state_ssm, cache_win_k, cache_win_v,
              norm_mix, w_in, conv_w, conv_b, dt_bias, a_log, d_skip, ssd_norm, att_norm, w_out,
              norm_ffn, router_w, router_b, w1, b1, w2, b2, norm_final):
    slopes = alibi_slopes()
    hp, hs = x_prompt, x_sample
    bp = x_prompt.shape[0]
    conv_p, ssm_p, k_p, v_p = [], [], [], []
    conv_s, ssm_s, k_s, v_s = [], [], [], []
    for l in range(DEPTH):
        mix_w = (w_in[l], conv_w[l], conv_b[l], dt_bias[l], a_log[l], d_skip[l], ssd_norm[l], att_norm[l], w_out[l])
        ffn_w = (router_w[l], router_b[l], w1[l], b1[l], w2[l], b2[l])
        zero_conv = jnp.zeros((bp, SSD_CONV - 1, CONV_DIM), hp.dtype)
        zero_ssm = jnp.zeros((bp, SSD_HEADS, SSD_HEAD_DIM, SSD_STATE), jnp.float32)
        m, c, s, k, v = token_mixer(rmsnorm(hp, norm_mix[l]), zero_conv, zero_ssm, None, None, slopes, *mix_w)
        hp = hp + m
        hp = hp + channel_mixer(rmsnorm(hp, norm_ffn[l]), *ffn_w)
        conv_p.append(c); ssm_p.append(s); k_p.append(k); v_p.append(v)
        m, c, s, k, v = token_mixer(rmsnorm(hs, norm_mix[l]), state_conv[l], state_ssm[l],
                                    cache_win_k[l], cache_win_v[l], slopes, *mix_w)
        hs = hs + m
        hs = hs + channel_mixer(rmsnorm(hs, norm_ffn[l]), *ffn_w)
        conv_s.append(c); ssm_s.append(s); k_s.append(k); v_s.append(v)
    y_prompt = rmsnorm(hp, norm_final)
    y_sample = rmsnorm(hs, norm_final)
    return (y_prompt, y_sample,
            jnp.stack(conv_p), jnp.stack(ssm_p), jnp.stack(k_p), jnp.stack(v_p),
            jnp.stack(conv_s), jnp.stack(ssm_s), jnp.stack(k_s), jnp.stack(v_s))


_drawn_inputs = setup_inputs


def setup_inputs(seed=0):
    import zlib

    import numpy as np

    out = dict(_drawn_inputs(seed))
    spreads = {}
    factors = {'b1': 8.0, 'b2': 8.0, 'norm_final': 2.903}
    for name, (base, spread) in spreads.items():
        noise = np.random.default_rng([zlib.crc32(name.encode()), seed]).standard_normal(out[name].shape)
        drawn = base * np.exp(spread * noise) if base else spread * noise
        out[name] = __import__('jax').numpy.asarray(drawn.astype(out[name].dtype))
    for name, factor in factors.items():
        out[name] = (out[name] * factor).astype(out[name].dtype)
    return out
```

```python
from contextlib import ExitStack

import numpy as np

import concourse.bass as bass
from concourse import mybir

F32 = mybir.dt.float32
I32 = mybir.dt.int32
U32 = mybir.dt.uint32
ALU = mybir.AluOpType
ACT = mybir.ActivationFunctionType
AX_X = mybir.AxisListType.X

P = 128
D = 1024
KT = D // P
SEQ = 256
DB, DT = 8, 4
NS = DB * DT
TOK = SEQ + NS
ROWS = [P, P, NS]
PAST = 1024
H, HP, N = 16, 64, 128
SSD = H * HP
G = 2
CONV = 4
CD = SSD + 2 * G * N
CT = CD // P
AH, AE = 8, 64
AW = AH * AE
MIX = SSD + AW
IN_W = SSD + CD + H + 3 * AW
NE, TOPK = 32, 4
F2 = 2 * D
LIMIT, ALPHA, EPS = 7.0, 1.702, 1e-5
PATTERNS = ((128, 1), (512, 4), (2048, 16))
NEG = -1e30

C = 64
MAX_PASS = -(-TOK // C)
SLOT = 2048
RING = 12
MIX_RING = 5

Z0, X0, B0_, C0_ = 0, SSD, 2 * SSD, 2 * SSD + G * N
DT0 = SSD + CD
Q0 = DT0 + H
K0, V0 = Q0 + AW, Q0 + 2 * AW
TILES = ([("q", i, Q0 + i * P) for i in range(4)] + [("k", i, K0 + i * P) for i in range(4)]
         + [("v", i, V0 + i * P) for i in range(4)] + [("x", i, X0 + i * P) for i in range(CT)]
         + [("z", i, Z0 + i * P) for i in range(8)])
NT = len(TILES)
NAT = [n for n, (kind, i, _) in enumerate(TILES) if kind in "kvz" or (kind == "x" and i < 10)]

XP = 3 + SEQ + DB * (3 + DT)
XS0 = 3 + SEQ
XC = XP - 3


def shape_constants():
    parts, at, pos = [], {}, 0

    def put(name, a):
        nonlocal pos
        a = np.asarray(a, np.float32)
        full = np.zeros((P, a.shape[1]), np.float32)
        full[:a.shape[0]] = a
        parts.append(full)
        at[name] = (pos, a.shape[1])
        pos += a.shape[1]

    r = np.arange(P)
    put("ident", np.eye(P))
    put("le", r[:, None] <= r[None, :])
    put("gt", r[:, None] > r[None, :])
    put("lt", r[:, None] < r[None, :])
    put("ones", np.ones((P, P)))
    put("slot", np.tile(r % C, (P, 1)))
    s = np.arange(NS)
    same = (s[:, None] // DT) == (s[None, :] // DT)
    put("le_s", (s[:, None] <= s[None, :]) & same)
    put("gt_s", (s[:, None] > s[None, :]) & same)
    put("same_s", same)
    put("expert", np.tile(np.arange(NE), (P, 1)))
    put("seq_of", (s[:, None] // DT) == np.arange(DB)[None, :])
    put("half", (r[:, None] // HP) == np.arange(2)[None, :])
    put("seq_cols", np.tile(((s[None, :] // DT) == np.arange(DB)[:, None]).reshape(1, -1), (P, 1)))
    row_h, row_t = (r % 32) // DT, r % DT
    put("head_of", row_h[:, None] == np.arange(AH)[None, :])
    tok = np.arange(NS)
    put("to_token", (tok[None, None, :] == DT * np.arange(DB)[None, :, None] + row_t[:, None, None])
        .reshape(P, -1))
    slopes = 2.0 ** (-8.0 * np.arange(1, AH + 1) / AH)

    def bias(h, d):
        count = sum(((d >= 0) & (d % dil == 0) & (d // dil <= w // dil)).astype(np.float64)
                    for w, dil in PATTERNS)
        return np.where(count > 0, -slopes[h] * d + np.log(np.maximum(count, 1)), NEG)

    used = (r % 32) < 2 * DT
    h_row = np.minimum(2 * (r // 32) + (r % 32) // DT, AH - 1)
    t_row = r % DT
    d_new = t_row[:, None, None] - (tok[None, None, :] % DT) + 0 * np.arange(DB)[None, :, None]
    own = (tok[None, None, :] // DT) == np.arange(DB)[None, :, None]
    new = np.where(own & (d_new >= 0), bias(h_row[:, None, None], d_new), NEG)
    put("bias_new", np.where(used[:, None, None], new, 0).reshape(P, -1))
    consts = np.concatenate(parts, 1)
    d_old = PAST + t_row[:, None] - np.arange(PAST)[None, :]
    bias_old = np.where(used[:, None], bias(h_row[:, None], d_old), 0).astype(np.float32)
    d_prompt = r[:, None, None] + P - np.arange(2 * P)[None, None, :] + 0 * np.arange(AH)[None, :, None]
    bias_prompt = bias(np.arange(AH)[None, :, None], d_prompt).astype(np.float32).reshape(P, -1)
    return consts, at, bias_old, bias_prompt


CONSTS, CONST_AT, BIAS_OLD, BIAS_PROMPT = shape_constants()


def mixer_steps():
    steps, nat = [], 0

    def proj(n):
        nonlocal nat
        steps.append(("proj", n))
        if n >= 1 and TILES[n - 1][0] == "x":
            steps.append(("conv", TILES[n - 1][1]))
        while nat < len(NAT) and NAT[nat] <= n - 2:
            steps.append(("nat", nat))
            nat += 1

    for n in range(12):
        proj(n)
    for b in range(DB):
        steps.append(("ktrans", b))
        if b:
            steps.append(("gather_o", b - 1))
        proj(12 + 2 * b)
        steps.append(("score", b))
        proj(13 + 2 * b)
        steps.append(("ptrans", b))
        steps.append(("pv", b))
    proj(28)
    steps.append(("gather_o", DB - 1))
    for n in range(29, NT):
        proj(n)
    while nat < len(NAT):
        steps.append(("nat", nat))
        nat += 1
    return steps


STEPS = mixer_steps()
NAT_ON_DVE = [i for i in range(len(NAT)) if i < 8 and i % 2 == 0]
NAT_ON_ACT = [i for i in range(len(NAT)) if i not in NAT_ON_DVE]


def ring_items():
    items = []
    for kind, i in STEPS:
        if kind == "proj" and i % 2 == 0:
            items.append(("w_in", i))
        if kind == "ktrans":
            items += [("k", i, 0), ("k", i, 1)]
        if kind == "ptrans":
            items += [("v", i, 0), ("v", i, 1)]
    return items + [("w_out", i) for i in range(MIX // P // 2)]


ITEMS = ring_items()
ITEM_AT = {item: n for n, item in enumerate(ITEMS)}


def hymba_step(nc, a, o):
    ctx = ExitStack()
    with ctx:
        sems = {}

        def sem(name):
            if name not in sems:
                sems[name] = ctx.enter_context(nc.semaphore(name))
            return sems[name]

        ring = ctx.enter_context(nc.sbuf_tensor("ring", [P, RING * SLOT], F32))
        WORDS = 28500
        own = ctx.enter_context(nc.sbuf_tensor("own", [P, WORDS], F32))
        ps = ctx.enter_context(nc.psum_tensor("ps", [P, 8, 512], F32))

        used = [0]

        def take(words):
            used[0] += words
            assert used[0] <= WORDS, used[0]
            return own[:, used[0] - words:used[0]]

        def sub(region, start, words):
            return region[:, start:start + words]

        def d3(ap, b):
            return ap.rearrange("p (a b) -> p a b", b=b)

        def d4(ap, b, c):
            return ap.rearrange("p (a b c) -> p a b c", b=b, c=c)

        consts = take(CONSTS.shape[1])

        def const(name, rows=P):
            start, n = CONST_AT[name]
            return consts[0:rows, start:start + n]

        ident = const("ident")
        h = d3(take(3 * D), D)
        r_xn = take(3 * D)
        xn = d3(r_xn, D)
        xs = xn
        r_xnT = take(KT * TOK)
        xnT = d3(r_xnT, TOK)
        r_xbcP = take(CT * XP)
        xbcP = d3(r_xbcP, XP)
        y = d3(sub(r_xbcP, 0, 3 * SSD), SSD)
        r_xbcT = take(CT * TOK)
        xbcT = d3(r_xbcT, TOK)
        mixT = d3(r_xbcT, TOK)
        r_qk = take(2 * 4 * TOK)
        qT = d3(sub(r_qk, 0, 4 * TOK), TOK)
        kT = d3(sub(r_qk, 4 * TOK, 4 * TOK), TOK)
        r_z = take(3 * SSD)
        z = d3(r_z, SSD)
        r_v = take(3 * AW)
        v = d3(r_v, AW)
        r_o = take(3 * AW)
        att = d3(r_o, AW)
        Bn = d3(take(3 * G * N), G * N)
        cw = d3(take(CT * 29), 29)
        w_dt = d3(take(KT * H), H)
        w_router = d3(take(KT * NE), NE)
        vecs = take(28)
        bvec = take(80)
        stat = take(64)
        st4 = take(32)
        dts = take(6 * 48)
        r_small = take(160)
        rows_small = take(128 + 80)

        work = ring[:, MIX_RING * SLOT:RING * SLOT]
        wk = [0]

        def work_take(words):
            wk[0] += words
            assert wk[0] <= (RING - MIX_RING) * SLOT
            return work[:, wk[0] - words:wk[0]]

        r_kTb = work_take(4 * PAST)
        kTb = d3(r_kTb, PAST)
        k_nat = d3(sub(r_kTb, 0, 3 * AW), AW)
        r_Qz = work_take(DB * 4 * 32)
        Qz = r_Qz.rearrange("p (b j c) -> p b j c", b=DB, j=4)
        r_PT = work_take(2 * 288)
        PTb = d3(r_PT, 288)
        r_OV = work_take(2 * 512)
        OVm = d3(r_OV, 512)
        conv_t = d3(work_take(2 * XC), XC)
        r_Pb = work_take(2 * 1056)
        Pb = d3(r_Pb, 1056)
        rows29 = r_Pb[:, 0:CD]
        bias_p = d3(work_take(AH * 2 * P), 2 * P)
        bias_o = work_take(PAST)
        utmp = d3(work_take(3 * TOK), TOK)
        PTp = d3(sub(r_OV, 0, 768), 384)
        Pp = d3(sub(r_Pb, 0, 768), 384)

        state = work[:, 0:DB * 8 * N].rearrange("p (b j n) -> p b j n", b=DB, j=8)
        w0 = DB * 8 * N
        stT = work[:, w0:w0 + SSD]
        tmp1 = work[:, w0 + SSD:w0 + 2 * SSD]
        Xh = work[:, w0 + 2 * SSD:w0 + 3 * SSD]
        Xd = work[:, w0 + 3 * SSD:w0 + 4 * SSD]
        dAm = [work[:, w0 + 4 * SSD + i * 512:w0 + 4 * SSD + (i + 1) * 512] for i in range(2)]
        Lb = [work[:, w0 + 4 * SSD + (2 + i) * 512:w0 + 4 * SSD + (3 + i) * 512] for i in range(2)]
        Mb = [sub(r_qk, i * 512, 512) for i in range(2)]
        dAx = sub(r_qk, 1024, SSD)
        fin_nat = dAx
        Bm = r_xnT[:, 0:G * DB * N].rearrange("p (g b n) -> p g b n", g=G, b=DB)
        St = sub(r_v, 0, SSD)
        GM = sub(r_v, SSD, 2 * P)
        conv_o3 = r_v
        conv_o_s = sub(r_qk, 0, CD)
        CTm = [sub(r_xnT, G * DB * N, DB * NS), sub(r_v, SSD + 2 * P, DB * NS)]
        ex = r_small[:, 0:48]
        edx = r_small[:, 48:112]
        cst = r_small[:, 112:144]

        xT = sub(r_xbcP, 0, 512)
        S1 = d3(sub(r_xbcP, 512, 192), 64)
        S2 = d3(sub(r_xbcP, 704, 384), 128)
        sel = sub(r_xbcP, 1088, 64)
        GT = sub(r_xbcP, 1152, TOK)
        xg, xl, sg, gg = (sub(r_xbcP, 1440 + i * 512, 512) for i in range(4))
        gT = sub(r_v, 0, 512)
        ysb = sub(r_v, 512, 512)
        cnt = sub(r_v, 1024, 256)
        b1s = sub(r_z, 0, F2)
        b2s = sub(r_z, F2, D)
        nfin = sub(r_o, 0, D)
        rt = sub(r_qk, 0, 2304)
        posm = d3(sub(rt, 0, 96), 32)
        gate = d3(sub(rt, 96, 96), 32)
        mask = d3(sub(rt, 192, 96), 32)
        logit = d3(sub(rt, 288, 96), 32)
        top8 = d3(sub(rt, 384, 24), 8)
        idx8 = d3(sub(rt, 408, 24), 8)
        idxf = d3(sub(rt, 432, 24), 8)
        e4 = d3(sub(rt, 456, 12), 4)
        rs1 = sub(rt, 468, 3)
        eq1 = sub(rt, 480, 32)
        passes = sub(rt, 512, 8)
        passes_i = rt[0:1, 520:521].bitcast(I32)

        def le(c):
            return const("le") if c < 2 else const("le_s", NS)

        def gt(c):
            return const("gt") if c < 2 else const("gt_s", NS)

        def same(c):
            return const("ones") if c < 2 else const("same_s", NS)

        def cols(c):
            return slice(P * c, P * c + ROWS[c])

        def stat2(hd, which):
            return st4[:, 8 * which + hd:8 * which + hd + 1]

        block = ctx.enter_context(nc.Block())

        def slot(n):
            return ring[:, n * SLOT:(n + 1) * SLOT]

        def mix_full(eng, item):
            n = ITEM_AT[item]
            eng.wait_ge(sem(f"slot_full{n % MIX_RING}"), 16 * (n // MIX_RING + 1))

        MIX_LOADS = [len([n for n in range(len(ITEMS)) if n % MIX_RING == s]) for s in range(MIX_RING)]

        def moe_slot(j):
            return (MIX_RING + j) % RING

        def moe_base(s):
            return 16 * MIX_LOADS[s] if s < MIX_RING else 0

        def wait_proj_out(eng, n):
            if n % 2 == 0:
                eng.wait_ge(sem("proj_out_act"), n // 2 + 1)
            else:
                eng.wait_ge(sem("proj_out_dve"), n // 2 + 1)

        def wait_nat_out(eng, i):
            if i in NAT_ON_DVE:
                eng.wait_ge(sem("nat_out_dve"), NAT_ON_DVE.index(i) + 1)
            else:
                eng.wait_ge(sem("nat_out_act"), NAT_ON_ACT.index(i) + 1)

        UT = [n for n in NAT if TILES[n][0] in "vz"]

        @block.sync
        def _(sp):
            sp.dma_start(h[:, 0:2, :], a["x_prompt"][0].rearrange("(i p) d -> p i d", p=P)).then_inc(sem("x_in"), 16)
            sp.dma_start(h[0:NS, 2, :], a["x_sample"].rearrange("b t d -> (b t) d")).then_inc(sem("x_in"), 16)
            w_in = a["w_in"][0].rearrange("(k p) c -> p k c", p=P)
            w_out = a["w_out"][0].rearrange("(k p) c -> p k c", p=P)
            for n, item in enumerate(ITEMS):
                s = n % MIX_RING
                if n >= MIX_RING:
                    sp.wait_ge(sem("slot_used"), n - MIX_RING + 1)
                if item[0] == "w_in":
                    c0 = TILES[item[1]][2]
                    dst, src = d3(slot(s), 2 * P), w_in[:, :, c0:c0 + 2 * P]
                elif item[0] == "w_out":
                    dst, src = d3(slot(s), D), w_out[:, 2 * item[1]:2 * item[1] + 2, :]
                else:
                    cache = a["cache_win_k" if item[0] == "k" else "cache_win_v"][0, item[1]]
                    src = cache.rearrange("(k p) h e -> p k (h e)", p=P)[:, 4 * item[2]:4 * item[2] + 4, :]
                    dst = d3(slot(s), AW)
                sp.dma_start(dst, src).then_inc(sem(f"slot_full{s}"), 16)
            sp.wait_ge(sem("work_free"), 1)
            sp.wait_ge(sem("ssm_s_out"), 16 * 8)
            w1 = a["w1"][0].rearrange("e (k p) c -> e k p c", p=P)
            w2 = a["w2"][0].rearrange("e (k p) c -> e p k c", p=P)

            def expert_loads(e, it):
                for j in range(RING):
                    s = moe_slot(j)
                    sp.wait_ge(sem("expert_slot_used"), it * RING + (j + 1))
                    if j < KT:
                        dst, src = slot(s), w1[bass.ds(e, 1), j].rearrange("e p c -> p (e c)")
                    else:
                        k2 = 2 * (j - KT)
                        dst, src = d3(slot(s), D), w2[bass.ds(e, 1), :, k2:k2 + 2].rearrange("e p k c -> p (e k) c")
                    sp.dma_start(dst, src).then_inc(sem(f"slot_full{s}"), 16)

            expert_loads(0, 0)
            with sp.Fori(1, NE) as e:
                expert_loads(e, e)
            sp.wait_ge(sem("passes_ready"), 1)
            npass = sp.value_load(passes_i, min_val=1, max_val=MAX_PASS)
            with sp.If(npass > 1):
                with sp.Fori(1, npass) as p:
                    with sp.Fori(0, NE) as e:
                        expert_loads(e, p * NE + e)

        @block.gpsimd
        def _(pool):
            pool.dma_start(rows29[0:24, :], a["state_conv"][0].rearrange("b t c -> (b t) c")).then_inc(sem("rows_in"), 16)
            pool.dma_start(rows29[24:28, :], a["conv_w"][0]).then_inc(sem("rows_in"), 16)
            pool.dma_start(rows29[28:29, :], a["conv_b"]).then_inc(sem("rows_in"), 16)
            nc.gpsimd.memset(xbcP[:, :, 0:3], 0.0).then_inc(sem("hist_zero"), 1)
            nc.gpsimd.memset(dts, 0.0).then_inc(sem("dts_zero"), 1)
            nc.gpsimd.memset(stat[:, 0:24], 1.0).then_inc(sem("stat_one"), 1)
            pool.wait_ge(sem("misc_ps"), 1)
            nc.gpsimd.memset(r_Qz, 0.0).then_inc(sem("qz_zero"), 1)

            for name, src, i0 in (("k", k_nat, 0), ("v", v, 4)):
                for i in range(i0, i0 + 4):
                    wait_nat_out(pool, i)
                pool.dma_start(o[name + "_prompt"].rearrange("(i p) h e -> p i (h e)", p=P), src[:, 0:2, :]).then_inc(sem(name + "_out"), 16)
                pool.dma_start(o[name + "_sample"].rearrange("t h e -> t (h e)"), src[0:NS, 2, :]).then_inc(sem(name + "_out"), 16)

            pool.wait_ge(sem("att_prompt_out"), 2)
            pool.wait_ge(sem("conv_out_ps"), 6)
            for b in range(DB):
                pool.dma_start(state[:, b], a["state_ssm"][0, b].rearrange("(j h) p n -> (h p) j n", j=8)).then_inc(sem(f"state_in{b}"), 16)
            pool.wait_ge(sem("conv_o_act"), 3)
            pool.wait_ge(sem("conv_o_dve"), 3)
            pool.dma_start(o["conv_prompt"], conv_o3[0:3, :]).then_inc(sem("conv_out"), 16)
            for b in range(DB):
                pool.dma_start(o["conv_sample"][b], conv_o_s[7 * b + 4:7 * b + 7, :]).then_inc(sem("conv_out"), 16)

            dA = dts[:, 48:96]
            dt = dts[:, 0:48]
            pool.wait_ge(sem("dt_ready"), 1)
            for i in range(8, 18):
                wait_nat_out(pool, i)
            batch = 0
            for c in range(3):
                n = ROWS[c]
                x3 = d3(xs[0:n, c, :], HP)
                if c >= 1:
                    pool.wait_ge(sem("st_ps"), c)
                nc.gpsimd.tensor_tensor(d3(Xh[0:n], HP), x3, dt[0:n, 16 * c:16 * c + 16].unsqueeze(2).broadcast_to([n, H, HP]),
                                        ALU.mult).then_inc(sem("X_ready"), 1)
                nc.gpsimd.tensor_tensor(d3(y[0:n, c, :], HP), x3, bvec[0:n, 32:48].unsqueeze(2).broadcast_to([n, H, HP]),
                                        ALU.mult).then_inc(sem("DX_ready"), 1)
                for hb in range(4):
                    if batch >= 2:
                        pool.wait_ge(sem("seg_ps"), batch - 1)
                    nc.gpsimd.tensor_tensor(
                        dAm[batch % 2].rearrange("p (h s) -> p h s", h=4)[0:n, :, 0:n],
                        gt(c).unsqueeze(1).broadcast_to([n, 4, n]),
                        dA[0:n, 16 * c + 4 * hb:16 * c + 4 * hb + 4].unsqueeze(2).broadcast_to([n, 4, n]),
                        ALU.mult).then_inc(sem("dAm_ready"), 1)
                    batch += 1
                pool.wait_ge(sem("X_ready"), c + 1)
                pool.wait_ge(sem("ex_ready"), c + 1)
                nc.gpsimd.tensor_tensor(d3(Xd[0:n], HP), d3(Xh[0:n], HP), ex[0:n, 0:16].unsqueeze(2).broadcast_to([n, H, HP]),
                                        ALU.mult).then_inc(sem("Xd_ready"), 1)
            for g in range(G):
                nc.gpsimd.tensor_tensor(Bm[0:NS, g], Bn[0:NS, 2, g * N:(g + 1) * N].unsqueeze(1).broadcast_to([NS, DB, N]),
                                        const("seq_of", NS).unsqueeze(2).broadcast_to([NS, DB, N]), ALU.mult).then_inc(sem("Bm_ready"), 1)
            for g in range(G):
                nc.gpsimd.tensor_tensor(d3(CTm[g], NS), xbcT[:, 10 + g, SEQ:TOK].unsqueeze(1).broadcast_to([P, DB, NS]),
                                        d3(const("seq_cols"), NS), ALU.mult).then_inc(sem("CTm_ready"), 1)
            pool.wait_ge(sem("fin_out"), 16)
            nc.gpsimd.tensor_copy(d3(dAx[0:NS], HP), dA[0:NS, 32:48].unsqueeze(2).broadcast_to([NS, H, HP])).then_inc(sem("dAx_ready"), 1)
            dst = o["ssm_sample"].rearrange("b (j h) p n -> (h p) b j n", j=8)
            for j in range(8):
                pool.wait_ge(sem("state_new"), j + 1)
                pool.dma_start(dst[:, :, j, :], state[:, :, j, :]).then_inc(sem("ssm_s_out"), 16)
            pool.wait_ge(sem("mixT_ps"), 12)
            nc.gpsimd.memset(GT, 0.0).then_inc(sem("GT_ready"), 1)
            nc.gpsimd.memset(ysb, 0.0).then_inc(sem("ysb_ready"), 1)
            pool.dma_start(b1s[0:NE, :], a["b1"][0]).then_inc(sem("bias_in"), 16)
            pool.dma_start(b2s[0:NE, :], a["b2"][0]).then_inc(sem("bias_in"), 16)
            pool.dma_start(nfin, a["norm_final"].partition_broadcast(P)).then_inc(sem("nfin_in"), 16)
            pool.wait_ge(sem("y_final"), 2)
            pool.dma_start(o["y_prompt"].rearrange("(i p) d -> p i d", p=P), h[:, 0:2, :]).then_inc(sem("y_out"), 16)
            pool.wait_ge(sem("y_final"), 3)
            pool.dma_start(o["y_sample"], h[0:NS, 2, :]).then_inc(sem("y_out"), 16)
            pool.wait_ge(sem("y_out"), 32)
            pool.wait_ge(sem("k_out"), 32)
            pool.wait_ge(sem("v_out"), 32)
            pool.wait_ge(sem("conv_out"), 16 * (DB + 1))
            pool.wait_ge(sem("fin_out"), 16)
            pool.wait_ge(sem("ssm_s_out"), 16 * 8)

        @block.scalar
        def _(act):
            act.dma_start(consts, a["consts"]).then_inc(sem("const_in"), 16)
            act.dma_start(rows_small[0:8, 0:P], a["norm_mix"][0].rearrange("(k p) -> k p", p=P)).then_inc(sem("vec_in"), 16)
            act.dma_start(rows_small[8:16, 0:P], a["norm_ffn"][0].rearrange("(k p) -> k p", p=P)).then_inc(sem("vec_in"), 16)
            act.dma_start(rows_small[16:24, 0:P], a["ssd_norm"][0].rearrange("(k p) -> k p", p=P)).then_inc(sem("vec_in"), 16)
            act.dma_start(rows_small[24:28, 0:P], a["att_norm"][0].rearrange("(k p) -> k p", p=P)).then_inc(sem("vec_in"), 16)
            for i, name in enumerate(("dt_bias", "a_log", "d_skip")):
                act.dma_start(rows_small[0:1, P + 16 * i:P + 16 * i + 16], a[name]).then_inc(sem("vec_in"), 16)
            act.dma_start(rows_small[0:1, P + 48:P + 80], a["router_b"]).then_inc(sem("vec_in"), 16)
            act.dma_start(w_dt, a["w_in"][0].rearrange("(k p) c -> p k c", p=P)[:, :, DT0:DT0 + H]).then_inc(sem("wdt_in"), 16)
            act.dma_start(w_router, a["router_w"][0].rearrange("(k p) c -> p k c", p=P)).then_inc(sem("wr_in"), 16)
            act.dma_start(bias_o, a["bias_old"]).then_inc(sem("bias_o_in"), 16)
            act.dma_start(bias_p, a["bias_prompt"].rearrange("p (h k) -> p h k", h=AH)).then_inc(sem("bias_p_in"), 16)

            def norm_rows(first):
                act.wait_ge(sem("ss_ready"), 3 * first + 3)
                nc.scalar.activation(stat[:, 16:19], stat[:, 0:3], ACT.Sqrt).then_inc(sem("rt_ready"), 1)
                act.wait_ge(sem("rstd_ready"), first + 1)
                for i in range(3):
                    n = ROWS[i]
                    nc.scalar.activation(xn[0:n, i, :], h[0:n, i, :], ACT.Copy, scale=stat[0:n, 20 + i:21 + i]).then_inc(sem("xn_ready"), 1)

            def xT_evac(first, g0):
                for k in range(1, KT, 2):
                    act.wait_ge(sem("xnT_ps"), first * KT + k + 1)
                    nc.scalar.activation(xnT[:, k, :], ps[:, k % 2, 0:TOK], ACT.Copy, scale=vecs[:, g0 + k:g0 + k + 1]).then_inc(sem("xnT_act"), 1)

            act.wait_ge(sem("bvec_ready"), 1)
            nc.scalar.activation(bvec[:, 16:32], bvec[:, 16:32], ACT.Exp).then_inc(sem("ea_ready"), 1)
            norm_rows(0)
            act.wait_ge(sem("vec_ready"), 1)
            xT_evac(0, 0)
            n_k = 0
            for kind, i in STEPS:
                if kind == "proj" and i % 2 == 0:
                    what, j, _ = TILES[i]
                    act.wait_ge(sem("proj_ps"), i // 2 + 1)
                    src = ps[:, i % 2, 0:TOK]
                    if what == "q":
                        nc.scalar.activation(qT[:, j, :], src, ACT.Copy, scale=AE ** -0.5).then_inc(sem("proj_out_act"), 1)
                    elif what == "k":
                        nc.scalar.activation(kT[:, j, :], src, ACT.Copy).then_inc(sem("proj_out_act"), 1)
                    elif what == "x":
                        nc.scalar.activation(xbcP[:, j, 3:XS0], src[:, 0:SEQ], ACT.Copy)
                        nc.scalar.activation(d3(xbcP[:, j, XS0:XP], 7)[:, :, 3:7], d3(src[:, SEQ:TOK], DT), ACT.Copy).then_inc(sem("proj_out_act"), 1)
                    else:
                        u = UT.index(i)
                        if u >= 3:
                            act.wait_ge(sem("nat_ps"), NAT.index(UT[u - 3]) + 1)
                        nc.scalar.activation(utmp[:, u % 3, :], src, ACT.Copy).then_inc(sem("proj_out_act"), 1)
                elif kind == "conv":
                    act.wait_ge(sem("conv_ready"), i + 1)
                    src = conv_t[:, i % 2, :]
                    nc.scalar.activation(xbcT[:, i, 0:SEQ], src[:, 0:SEQ], ACT.Silu)
                    nc.scalar.activation(d3(xbcT[:, i, SEQ:TOK], DT), d3(src[:, SEQ:XC], 7)[:, :, 3:7], ACT.Silu).then_inc(sem("silu_ready"), 1)
                elif kind == "nat" and i in NAT_ON_ACT:
                    what, j, _ = TILES[NAT[i]]
                    act.wait_ge(sem("nat_ps"), i + 1)
                    func = ACT.Silu if what == "z" else ACT.Copy
                    dst, j = {"k": (k_nat, j), "v": (v, j), "z": (z, j), "x": (xs, j)}[what]
                    if what == "x" and j >= 8:
                        dst, j = Bn, j - 8
                    nc.scalar.activation(dst[:, 0:2, j * P:(j + 1) * P], d3(ps[:, 2, 0:2 * P], P), func)
                    nc.scalar.activation(dst[0:NS, 2, j * P:(j + 1) * P], ps[0:NS, 2, 2 * P:3 * P], func).then_inc(sem("nat_out_act"), 1)
                elif kind == "ktrans":
                    if i == 0:
                        act.wait_ge(sem("k_out"), 32)
                    for q in range(0, 8, 2):
                        half, j = q // 4, q % 4
                        act.wait_ge(sem("ktrans_ps"), 6 * i + 3 * half + j + 1)
                        nc.scalar.activation(kTb[:, j, 512 * half:512 * half + 512], ps[:, 4 + q % 2, :], ACT.Copy).then_inc(sem("ktrans_act"), 1)
                elif kind == "score":
                    act.wait_ge(sem("score_biased"), i + 1)
                    nc.scalar.activation(Pb[:, i % 2, :], Pb[:, i % 2, :], ACT.Exp, bias=stat[:, 32 + i:33 + i],
                                         accum_out=stat[:, 40 + i:41 + i]).then_inc(sem("score_exp"), 1)
                elif kind == "ptrans":
                    act.wait_ge(sem("ptrans_ps"), i + 1)
                    nc.scalar.activation(PTb[:, i % 2, 0:128].rearrange("p (k j c) -> p k j c", k=4, j=4),
                                         ps[:, 4, :].rearrange("p (k j c) -> p k j c", k=4, j=4)[:, :, :, 0:8], ACT.Copy).then_inc(sem("PT_act"), 1)

            act.wait_ge(sem("dt_abs"), 1)
            nc.scalar.activation(dts[:, 144:192], dts[:, 96:144], ACT.Exp, scale=-1.0).then_inc(sem("dt_exp"), 1)
            act.wait_ge(sem("dt_one"), 1)
            nc.scalar.activation(dts[:, 192:240], dts[:, 96:144], ACT.Ln).then_inc(sem("dt_ln"), 1)

            for hd in range(AH):
                act.wait_ge(sem("ps_biased"), hd + 1)
                nc.scalar.activation(Pp[:, hd % 2, 0:P], Pp[:, hd % 2, 0:P], ACT.Exp, bias=stat2(hd, 0), accum_out=stat2(hd, 2))
                nc.scalar.activation(Pp[:, hd % 2, P:3 * P], Pp[:, hd % 2, P:3 * P], ACT.Exp, bias=stat2(hd, 1), accum_out=stat2(hd, 3)).then_inc(sem("pp_exp"), 1)
                act.wait_ge(sem("ppT_ps"), hd + 1)
                nc.scalar.activation(PTp[:, hd % 2, :], ps[:, 6 + hd % 2, 0:3 * P], ACT.Copy).then_inc(sem("ppT_act"), 1)

            for q in range(3):
                act.wait_ge(sem("conv_out_ps"), 2 * q + 2)
                nc.scalar.activation(conv_o_s[0:DB * 7, 512 * q:512 * q + 512], ps[0:DB * 7, 4 + 2 * (q % 2) + 1, :], ACT.Copy).then_inc(sem("conv_o_act"), 1)

            batch = 0
            for c in range(3):
                n = ROWS[c]
                act.wait_ge(sem("cs_ready"), c + 1)
                nc.scalar.activation(ex[0:n], ex[0:n], ACT.Exp).then_inc(sem("ex_ready"), 1)
                for hb in range(4):
                    act.wait_ge(sem("seg_ps"), batch + 1)
                    if batch >= 2:
                        act.wait_ge(sem("M_ready"), batch - 1)
                    nc.scalar.activation(d3(Lb[batch % 2], P)[0:n, :, 0:n], d3(ps[:, 2 + batch % 2, :], P)[0:n, :, 0:n], ACT.Exp).then_inc(sem("L_ready"), 1)
                    batch += 1
                if c == 1:
                    act.wait_ge(sem("fin_ps"), 1)
                    act.wait_ge(sem("conv_out"), 16 * (DB + 1))
                    nc.scalar.activation(fin_nat, ps[:, 6:8, :].rearrange("p a b -> p (a b)"), ACT.Copy).then_inc(sem("fin_ready"), 1)
                    act.wait_ge(sem("fin_ready"), 1)
                    act.dma_start(o["ssm_prompt"].rearrange("(j h) p n -> (h p) j n", j=8), d3(fin_nat, N)).then_inc(sem("fin_out"), 16)
            for b in range(DB):
                act.wait_ge(sem("stT_ps"), b + 1)
                nc.scalar.activation(stT, ps[:, 0:2, :].rearrange("p a b -> p (a b)"), ACT.Copy).then_inc(sem("stT_ready"), 1)
            act.wait_ge(sem("decay_ps"), 1)
            nc.scalar.activation(edx, ps[:, 2, 0:64], ACT.Exp).then_inc(sem("edx_ready"), 1)

            act.wait_ge(sem("mix_ss"), 1)
            nc.scalar.activation(dts[:, 0:9], stat[:, 0:9], ACT.Sqrt).then_inc(sem("mix_rt"), 1)
            act.wait_ge(sem("mix_rstd"), 1)
            for c in range(3):
                n = ROWS[c]
                for g in range(G):
                    nc.scalar.activation(y[0:n, c, 512 * g:512 * g + 512], y[0:n, c, 512 * g:512 * g + 512], ACT.Copy, scale=dts[0:n, 16 + 3 * c + g:17 + 3 * c + g])
                nc.scalar.activation(att[0:n, c, :], att[0:n, c, :], ACT.Copy, scale=dts[0:n, 18 + 3 * c:19 + 3 * c]).then_inc(sem("mix_ready"), 1)
            for k in range(1, 12, 2):
                act.wait_ge(sem("mixT_ps"), k + 1)
                nc.scalar.activation(mixT[:, k, :], ps[:, k % 2, 0:TOK], ACT.Copy, scale=vecs[:, 16 + k:17 + k]).then_inc(sem("mixT_act"), 1)

            norm_rows(1)
            xT_evac(1, 8)
            act.wait_ge(sem("top_ready"), 1)
            for i in range(3):
                n = ROWS[i]
                ins = nc.scalar.activation(e4[0:n, i, :], top8[0:n, i, 0:4], ACT.Exp, bias=rs1[0:n, i:i + 1])
            ins.then_inc(sem("e4_ready"), 1)

            act.wait_ge(sem("passes_ready"), 1)
            npass = act.value_load(passes_i, min_val=1, max_val=MAX_PASS)
            with act.Fori(0, npass) as p:
                with act.Fori(0, NE) as e:
                    it = p * NE + e
                    act.wait_ge(sem("glu_ready"), it + 1)
                    nc.scalar.activation(sg, xg, ACT.Sigmoid, scale=ALPHA).then_inc(sem("sig_ready"), 1)
                    act.wait_ge(sem("GT_ps"), it + 2)
                    nc.scalar.activation(GT, ps[:, 5, 0:TOK], ACT.Copy).then_inc(sem("GT_ready"), 1)
                    act.wait_ge(sem("gT_ps"), it + 1)
                    nc.scalar.activation(gT, ps[:, 3, :], ACT.Copy).then_inc(sem("gT_ready"), 1)
                    act.wait_ge(sem("expert_slot_used"), RING * it + 2 * RING)
                    nc.scalar.activation(ysb, ps[:, 4, :], ACT.Copy).then_inc(sem("ysb_ready"), 1)

            act.wait_ge(sem("ss_ready"), 9)
            nc.scalar.activation(stat[:, 16:19], stat[:, 0:3], ACT.Sqrt).then_inc(sem("rt_ready"), 1)

        @block.vector
        def _(dve):
            chain = [0]

            def link(ins):
                chain[0] += 1
                ins.then_inc(sem("dve_link"), 1)
                dve.wait_ge(sem("dve_link"), chain[0])

            def both(bank):
                return ps[:, bank:bank + 2, :].rearrange("p a b -> p (a b)")

            def row_sums(call):
                for i in range(3):
                    n = ROWS[i]
                    nc.vector.tensor_tensor_reduce(xn[0:n, i, :], h[0:n, i, :], h[0:n, i, :], 1.0 / D, EPS,
                                                   ALU.mult, ALU.add, stat[0:n, i:i + 1]).then_inc(sem("ss_ready"), 1)

            def row_rstd(call):
                dve.wait_ge(sem("rt_ready"), call + 1)
                nc.vector.reciprocal(stat[:, 20:23], stat[:, 16:19]).then_inc(sem("rstd_ready"), 1)

            def xT_evac(call, g0):
                for k in range(0, KT, 2):
                    dve.wait_ge(sem("xnT_ps"), call * KT + k + 1)
                    nc.vector.tensor_scalar(xnT[:, k, :], ps[:, k % 2, 0:TOK], vecs[:, g0 + k:g0 + k + 1], None, ALU.mult).then_inc(sem("xnT_dve"), 1)

            dve.wait_ge(sem("stat_one"), 1)
            dve.wait_ge(sem("x_in"), 32)
            row_sums(0)
            dve.wait_ge(sem("misc_ps"), 1)
            nc.vector.tensor_copy(vecs, ps[:, 7, 0:28]).then_inc(sem("vec_ready"), 1)
            nc.vector.tensor_copy(bvec, ps[:, 7, 32:112]).then_inc(sem("bvec_ready"), 1)
            link(nc.vector.tensor_copy(cw, d3(ps[:, 6, 0:CT * 29], 29)))
            for i in range(CT):
                ins = nc.vector.tensor_copy(d3(xbcP[:, i, XS0:XP], 7)[:, :, 0:3], d3(cw[:, i, 0:24], 3))
            link(ins)
            row_rstd(0)
            dve.wait_ge(sem("ea_ready"), 1)
            link(nc.vector.tensor_scalar(bvec[:, 16:32], bvec[:, 16:32], -1.0, None, ALU.mult))
            xT_evac(0, 0)
            dve.wait_ge(sem("hist_zero"), 1)
            for kind, i in STEPS:
                if kind == "proj" and i % 2 == 1:
                    what, j, _ = TILES[i]
                    dve.wait_ge(sem("slot_used"), ITEM_AT[("w_in", i - 1)] + 1)
                    src = ps[:, i % 2, 0:TOK]
                    if what == "q":
                        nc.vector.tensor_scalar(qT[:, j, :], src, AE ** -0.5, None, ALU.mult).then_inc(sem("proj_out_dve"), 1)
                    elif what == "k":
                        nc.vector.tensor_copy(kT[:, j, :], src).then_inc(sem("proj_out_dve"), 1)
                    elif what == "x":
                        nc.vector.tensor_copy(xbcP[:, j, 3:XS0], src[:, 0:SEQ])
                        nc.vector.tensor_copy(d3(xbcP[:, j, XS0:XP], 7)[:, :, 3:7], d3(src[:, SEQ:TOK], DT)).then_inc(sem("proj_out_dve"), 1)
                    else:
                        u = UT.index(i)
                        if u >= 3:
                            dve.wait_ge(sem("nat_ps"), NAT.index(UT[u - 3]) + 1)
                        nc.vector.tensor_copy(utmp[:, u % 3, :], src).then_inc(sem("proj_out_dve"), 1)
                    if i == 3:
                        dve.wait_ge(sem("qz_zero"), 1)
                        wait_proj_out(dve, 2)
                        wait_proj_out(dve, 3)
                        for j in range(4):
                            nc.vector.tensor_tensor(
                                Qz[:, :, j, 0:8].rearrange("p b (u t) -> p b u t", u=2),
                                d3(qT[:, j, SEQ:TOK], DT).unsqueeze(2).broadcast_to([P, DB, 2, DT]),
                                const("half").unsqueeze(1).unsqueeze(3).broadcast_to([P, DB, 2, DT]),
                                ALU.mult).then_inc(sem("Qz_ready"), 1)
                elif kind == "conv":
                    wait_proj_out(dve, 12 + i)
                    if i >= 2:
                        dve.wait_ge(sem("silu_ready"), i - 1)
                    t = conv_t[:, i % 2, :]
                    link(nc.vector.tensor_scalar(t, xbcP[:, i, 0:XC], cw[:, i, 24:25], cw[:, i, 28:29], ALU.mult, ALU.add))
                    for k in range(1, CONV):
                        ins = nc.vector.scalar_tensor_tensor(t, xbcP[:, i, k:k + XC], cw[:, i, 24 + k:25 + k], t, ALU.mult, ALU.add)
                        if k < CONV - 1:
                            link(ins)
                    ins.then_inc(sem("conv_ready"), 1)
                elif kind == "nat" and i in NAT_ON_DVE:
                    what, j, _ = TILES[NAT[i]]
                    dve.wait_ge(sem("nat_ps"), i + 1)
                    dst = {"k": k_nat, "v": v}[what]
                    nc.vector.tensor_copy(dst[:, 0:2, j * P:(j + 1) * P], d3(ps[:, 2, 0:2 * P], P))
                    nc.vector.tensor_copy(dst[0:NS, 2, j * P:(j + 1) * P], ps[0:NS, 2, 2 * P:3 * P]).then_inc(sem("nat_out_dve"), 1)
                elif kind == "ktrans":
                    if i == 0:
                        dve.wait_ge(sem("k_out"), 32)
                    for q in range(1, 8, 2):
                        half, j = q // 4, q % 4
                        if j < 3:
                            dve.wait_ge(sem("ktrans_ps"), 6 * i + 3 * half + j + 1)
                        else:
                            dve.wait_ge(sem("slot_used"), ITEM_AT[("k", i, half)] + 1)
                        nc.vector.tensor_copy(kTb[:, j, 512 * half:512 * half + 512], ps[:, 4 + q % 2, :]).then_inc(sem("ktrans_dve"), 1)
                elif kind == "score":
                    dve.wait_ge(sem("score_ps"), i + 1)
                    if i == 0:
                        dve.wait_ge(sem("bias_o_in"), 16)
                    nc.vector.tensor_tensor_reduce(Pb[:, i % 2, 0:PAST], both(6), bias_o, 1.0, NEG, ALU.add, ALU.max, stat[:, 24:25]).then_inc(sem("smax"), 1)
                    nc.vector.tensor_tensor_reduce(Pb[:, i % 2, PAST:PAST + NS], ps[:, 3, 0:NS], const("bias_new")[:, NS * i:NS * i + NS], 1.0, NEG,
                                                   ALU.add, ALU.max, stat[:, 25:26]).then_inc(sem("smax"), 1)
                    dve.wait_ge(sem("smax"), 2 * i + 2)
                    link(nc.vector.tensor_tensor(stat[:, 26:27], stat[:, 24:25], stat[:, 25:26], ALU.max))
                    nc.vector.tensor_scalar(stat[:, 32 + i:33 + i], stat[:, 26:27], -1.0, None, ALU.mult).then_inc(sem("score_biased"), 1)
                    dve.wait_ge(sem("score_exp"), i + 1)
                    link(nc.vector.reciprocal(stat[:, 48 + i:49 + i], stat[:, 40 + i:41 + i]))
                    nc.vector.tensor_scalar(Pb[:, i % 2, :], Pb[:, i % 2, :], stat[:, 48 + i:49 + i], None, ALU.mult).then_inc(sem("P_ready"), 1)
                elif kind == "ptrans":
                    dve.wait_ge(sem("ptrans_ps"), i + 1)
                    nc.vector.tensor_copy(PTb[:, i % 2, 128:256].rearrange("p (k j c) -> p k j c", k=4, j=4),
                                          ps[:, 5, :].rearrange("p (k j c) -> p k j c", k=4, j=4)[:, :, :, 0:8])
                    nc.vector.tensor_copy(d3(PTb[0:NS, i % 2, 256:288], 8), d3(ps[0:NS, 3, 128:256], 32)[:, :, 0:8]).then_inc(sem("PT_dve"), 1)
                elif kind == "pv":
                    dve.wait_ge(sem("pv_ps"), i + 1)
                    nc.vector.tensor_tensor(d3(OVm[:, i % 2, :], AE), d3(ps[:, 6, :], AE), const("head_of").unsqueeze(2).broadcast_to([P, AH, AE]),
                                            ALU.mult).then_inc(sem("OV_ready"), 1)
                elif kind == "gather_o":
                    dve.wait_ge(sem("go_ps"), i + 1)
                    if i == 0:
                        nc.vector.tensor_copy(att[0:NS, 2, :], ps[0:NS, 3, :]).then_inc(sem("att_s"), 1)
                    else:
                        dve.wait_ge(sem("att_s"), i)
                        nc.vector.tensor_tensor(att[0:NS, 2, :], ps[0:NS, 3, :], att[0:NS, 2, :], ALU.add).then_inc(sem("att_s"), 1)

            raw, dt, dA = dts[:, 240:288], dts[:, 0:48], dts[:, 48:96]
            u1, e1, ln1 = dts[:, 96:144], dts[:, 144:192], dts[:, 192:240]
            dve.wait_ge(sem("dts_zero"), 1)
            dve.wait_ge(sem("dt_ps"), 1)
            link(nc.vector.tensor_tensor(d3(raw[:, 0:32], H), d3(ps[:, 3, 0:32], H), bvec[:, 0:16].unsqueeze(1).broadcast_to([P, 2, H]), ALU.add))
            link(nc.vector.tensor_tensor(raw[0:NS, 32:48], ps[0:NS, 3, 32:48], bvec[0:NS, 0:16], ALU.add))
            link(nc.vector.tensor_scalar(u1, raw, -1.0, None, ALU.mult))
            nc.vector.tensor_tensor(u1, u1, raw, ALU.max).then_inc(sem("dt_abs"), 1)
            dve.wait_ge(sem("dt_exp"), 1)
            nc.vector.tensor_scalar(u1, e1, 1.0, None, ALU.add).then_inc(sem("dt_one"), 1)
            dve.wait_ge(sem("dt_one"), 1)
            link(nc.vector.tensor_scalar(dt, u1, -1.0, None, ALU.add))
            link(nc.vector.tensor_scalar(dA, dt, 0.0, None, ALU.is_equal))
            link(nc.vector.tensor_tensor(dt, dt, dA, ALU.add))
            link(nc.vector.tensor_tensor(dA, dA, e1, ALU.mult))
            dve.wait_ge(sem("dt_ln"), 1)
            link(nc.vector.reciprocal(u1, dt))
            link(nc.vector.tensor_tensor(u1, u1, e1, ALU.mult))
            link(nc.vector.tensor_tensor(u1, u1, ln1, ALU.mult))
            link(nc.vector.tensor_tensor(u1, u1, dA, ALU.add))
            link(nc.vector.scalar_tensor_tensor(dt, raw, 0.0, u1, ALU.max, ALU.add))
            nc.vector.tensor_tensor(d3(dA, H), d3(dt, H), bvec[:, 16:32].unsqueeze(1).broadcast_to([P, 3, H]), ALU.mult).then_inc(sem("dt_ready"), 1)

            dve.wait_ge(sem("bias_p_in"), 16)
            for hd in range(AH):
                dve.wait_ge(sem("pps_ps"), hd + 1)
                if hd >= 2:
                    dve.wait_ge(sem("ppT_ps"), hd - 1)
                bank = 4 + hd % 2
                dve.wait_ge(sem("ps_biased"), hd)
                nc.vector.tensor_tensor_reduce(Pp[:, hd % 2, 0:P], ps[:, bank, 0:P], bias_p[:, hd, P:2 * P], 1.0, NEG,
                                               ALU.add, ALU.max, stat[:, 24:25]).then_inc(sem("pmax"), 1)
                nc.vector.tensor_tensor_reduce(Pp[:, hd % 2, P:3 * P], ps[:, bank, P:3 * P], bias_p[:, hd, :], 1.0, NEG,
                                               ALU.add, ALU.max, stat[:, 25:26]).then_inc(sem("pmax"), 1)
                dve.wait_ge(sem("pmax"), 2 * hd + 2)
                link(nc.vector.tensor_scalar(stat2(hd, 0), stat[:, 24:25], -1.0, None, ALU.mult))
                nc.vector.tensor_scalar(stat2(hd, 1), stat[:, 25:26], -1.0, None, ALU.mult).then_inc(sem("ps_biased"), 1)
            dve.wait_ge(sem("pav_ps"), 1)
            link(nc.vector.reciprocal(st4[:, 16:32], st4[:, 16:32]))
            for i in range(2):
                nc.vector.tensor_tensor(d3(att[:, i, :], AE), d3(ps[:, i, :], AE), st4[:, 16 + 8 * i:24 + 8 * i].unsqueeze(2).broadcast_to([P, AH, AE]),
                                        ALU.mult).then_inc(sem("att_prompt_out"), 1)
            dve.wait_ge(sem("att_prompt_out"), 2)
            for i in range(3):
                n = ROWS[i]
                link(nc.vector.tensor_tensor_reduce(tmp1[0:n, 0:AW], att[0:n, i, :], att[0:n, i, :], 1.0 / AW, EPS,
                                                    ALU.mult, ALU.add, stat[0:n, 3 * i + 2:3 * i + 3]))

            dve.wait_ge(sem("v_out"), 32)
            for q in range(3):
                dve.wait_ge(sem("conv_out_ps"), 2 * q + 1)
                nc.vector.tensor_copy(conv_o3[0:3, 512 * q:512 * q + 512], ps[0:3, 4 + 2 * (q % 2), :]).then_inc(sem("conv_o_dve"), 1)

            dve.wait_ge(sem("conv_out"), 16 * (DB + 1))
            for c in range(3):
                n = ROWS[c]
                dve.wait_ge(sem("gram_ps"), c + 1)
                link(nc.vector.tensor_tensor(d3(GM, P)[0:n, :, 0:n], d3(ps[:, 0, 0:2 * P], P)[0:n, :, 0:n],
                                             le(c).unsqueeze(1).broadcast_to([n, G, n]), ALU.mult))
                if c >= 1:
                    dve.wait_ge(sem("Xd_ready"), c)
                link(nc.vector.tensor_copy(ex[0:n, 16:48], ps[0:n, 1, 0:32]))
                nc.vector.tensor_tensor(ex[0:n, 0:16], ex[0:n, 32:48], ex[0:n, 16:32], ALU.subtract).then_inc(sem("cs_ready"), 1)
                for hb in range(4):
                    batch = 4 * c + hb
                    dve.wait_ge(sem("L_ready"), batch + 1)
                    if batch >= 2:
                        dve.wait_ge(sem("yd_ps"), batch - 1)
                    nc.vector.tensor_tensor(d3(Mb[batch % 2], P)[0:n, :, 0:n], d3(Lb[batch % 2], P)[0:n, :, 0:n],
                                            GM[0:n, (hb // 2) * P:(hb // 2) * P + n].unsqueeze(1).broadcast_to([n, 4, n]),
                                            ALU.mult).then_inc(sem("M_ready"), 1)
                yc = y[0:n, c, :]
                dve.wait_ge(sem("yd_ps"), 4 * c + 4)
                dve.wait_ge(sem("DX_ready"), c + 1)
                nc.vector.tensor_tensor(yc, yc, both(4)[0:n], ALU.add).then_inc(sem("yd_out"), 1)
                dve.wait_ge(sem("yd_out"), c + 1)
                if c >= 1:
                    dve.wait_ge(sem("yo_ps"), c)
                    dve.wait_ge(sem("ex_ready"), c + 1)
                    nc.vector.tensor_tensor(d3(tmp1[0:n], HP), d3(both(6)[0:n], HP), ex[0:n, 16:32].unsqueeze(2).broadcast_to([n, H, HP]),
                                            ALU.mult).then_inc(sem("yo_out"), 1)
                    dve.wait_ge(sem("yo_out"), c)
                    link(nc.vector.tensor_tensor(yc, yc, tmp1[0:n], ALU.add))
                if c == 0:
                    dve.wait_ge(sem("st_ps"), 1)
                    nc.vector.tensor_copy(St, both(6)).then_inc(sem("St_ready"), 1)
                if c == 1:
                    dve.wait_ge(sem("st_ps"), 2)
                    link(nc.vector.tensor_tensor(d3(St, HP), d3(St, HP), ex[:, 32:48].unsqueeze(2).broadcast_to([P, H, HP]), ALU.mult))
                    nc.vector.tensor_tensor(St, St, both(6), ALU.add).then_inc(sem("St_ready"), 1)
                if c == 0:
                    wait_nat_out(dve, len(NAT) - 1)
                link(nc.vector.tensor_tensor(yc, yc, z[0:n, c, :], ALU.mult))
                for g in range(G):
                    link(nc.vector.tensor_tensor_reduce(tmp1[0:n, 0:512], yc[:, 512 * g:512 * g + 512], yc[:, 512 * g:512 * g + 512], 1.0 / 512, EPS,
                                                        ALU.mult, ALU.add, stat[0:n, 3 * c + g:3 * c + g + 1]))
            dve.wait_ge(sem("edx_ready"), 1)
            for j in range(8):
                dve.wait_ge(sem("fs_ps"), j + 1)
                dve.wait_ge(sem("state_new"), j)
                link(nc.vector.tensor_tensor(d3(tmp1, N), state[:, :, j, :], edx[:, 8 * j:8 * j + 8].unsqueeze(2).broadcast_to([P, DB, N]), ALU.mult))
                nc.vector.tensor_tensor(state[:, :, j, :], d3(tmp1, N), d3(both(4 + 2 * (j % 2)), N), ALU.add).then_inc(sem("state_new"), 1)
            dve.wait_ge(sem("state_new"), 8)
            nc.vector.tensor_copy(stat[:, 27:28], stat[:, 0:1]).then_inc(sem("work_free"), 1)
            nc.vector.tensor_copy(stat[:, 28:29], stat[:, 0:1]).then_inc(sem("mix_ss"), 1)
            dve.wait_ge(sem("mix_rt"), 1)
            nc.vector.reciprocal(dts[:, 16:25], dts[:, 0:9]).then_inc(sem("mix_rstd"), 1)
            for k in range(0, 12, 2):
                dve.wait_ge(sem("mixT_ps"), k + 1)
                nc.vector.tensor_scalar(mixT[:, k, :], ps[:, k % 2, 0:TOK], vecs[:, 16 + k:17 + k], None, ALU.mult).then_inc(sem("mixT_dve"), 1)

            dve.wait_ge(sem("expert_slot_used"), RING)
            nc.vector.tensor_tensor(h[:, 0, :], h[:, 0, :], both(2), ALU.add)
            nc.vector.tensor_tensor(h[:, 1, :], h[:, 1, :], both(4), ALU.add)
            nc.vector.tensor_tensor(h[0:NS, 2, 0:512], h[0:NS, 2, 0:512], ps[0:NS, 6, :], ALU.add)
            link(nc.vector.tensor_tensor(h[0:NS, 2, 512:D], h[0:NS, 2, 512:D], ps[NS:2 * NS, 6, :], ALU.add))
            row_sums(1)
            row_rstd(1)
            xT_evac(1, 8)

            dve.wait_ge(sem("logit_ps"), 1)
            nc.vector.tensor_tensor(logit[:, 0:2, :], d3(ps[:, 2, 0:2 * NE], NE), bvec[:, 48:80].unsqueeze(1).broadcast_to([P, 2, NE]), ALU.add)
            link(nc.vector.tensor_tensor(logit[0:NS, 2, :], ps[0:NS, 2, 2 * NE:3 * NE], bvec[0:NS, 48:80], ALU.add))
            for i in range(3):
                ins = nc.vector.max(top8[0:ROWS[i], i, :], logit[0:ROWS[i], i, :])
            link(ins)
            for i in range(3):
                n = ROWS[i]
                nc.vector.max_index(idx8[0:n, i, :].bitcast(U32), top8[0:n, i, :], logit[0:n, i, :])
                ins = nc.vector.tensor_scalar(rs1[0:n, i:i + 1], top8[0:n, i, 0:1], -1.0, None, ALU.mult)
            ins.then_inc(sem("top_ready"), 1)
            dve.wait_ge(sem("top_ready"), 1)
            for i in range(3):
                ins = nc.vector.tensor_copy(idxf[0:ROWS[i], i, :], idx8[0:ROWS[i], i, :].bitcast(U32))
            link(ins)
            dve.wait_ge(sem("e4_ready"), 1)
            for i in range(3):
                n = ROWS[i]
                ins = nc.vector.tensor_reduce(rs1[0:n, i:i + 1], e4[0:n, i, :], AX_X, ALU.add)
            link(ins)
            for i in range(3):
                ins = nc.vector.reciprocal(rs1[0:ROWS[i], i:i + 1], rs1[0:ROWS[i], i:i + 1])
            link(ins)
            for i in range(3):
                n = ROWS[i]
                ins = nc.vector.tensor_scalar(e4[0:n, i, :], e4[0:n, i, :], rs1[0:n, i:i + 1], None, ALU.mult)
            link(ins)
            for i in range(3):
                n = ROWS[i]
                expert = const("expert", n)
                for j in range(TOPK):
                    pick, weight = idxf[0:n, i, j:j + 1], e4[0:n, i, j:j + 1]
                    if j == 0:
                        nc.vector.tensor_scalar(mask[0:n, i, :], expert, pick, None, ALU.is_equal)
                        link(nc.vector.tensor_scalar(gate[0:n, i, :], expert, pick, weight, ALU.is_equal, ALU.mult))
                    else:
                        link(nc.vector.tensor_scalar(eq1[0:n], expert, pick, None, ALU.is_equal))
                        nc.vector.tensor_tensor(mask[0:n, i, :], mask[0:n, i, :], eq1[0:n], ALU.add)
                        link(nc.vector.scalar_tensor_tensor(gate[0:n, i, :], eq1[0:n], weight, gate[0:n, i, :], ALU.mult, ALU.add))
            nc.vector.tensor_copy(stat[:, 27:28], stat[:, 0:1]).then_inc(sem("mask_ready"), 1)
            dve.wait_ge(sem("pos_ps"), 1)
            nc.vector.scalar_tensor_tensor(posm[:, 0:2, :], d3(ps[:, 3, 0:2 * NE], NE), 1.0, mask[:, 0:2, :], ALU.add, ALU.mult)
            link(nc.vector.scalar_tensor_tensor(posm[0:NS, 2, :], ps[0:NS, 3, 2 * NE:3 * NE], 1.0, mask[0:NS, 2, :], ALU.add, ALU.mult))
            nc.vector.tensor_scalar(posm[:, 0:2, :], posm[:, 0:2, :], -1.0, None, ALU.add).then_inc(sem("pos_shifted"), 1)
            nc.vector.tensor_scalar(posm[0:NS, 2, :], posm[0:NS, 2, :], -1.0, None, ALU.add).then_inc(sem("pos_shifted"), 1)
            link(nc.vector.tensor_reduce(passes[0:1, 0:1], ps[0:1, 3, 3 * NE:4 * NE], AX_X, ALU.max))
            nc.vector.tensor_copy(stat[:, 28:29], stat[:, 0:1]).then_inc(sem("hid_read"), 1)
            nc.vector.tensor_copy(stat[:, 29:30], stat[:, 0:1]).then_inc(sem("comb_read"), 4)
            for k in range(1, MAX_PASS):
                ins = nc.vector.tensor_scalar(passes[0:1, k:k + 1], passes[0:1, 0:1], float(C * k), None, ALU.is_gt)
            link(ins)
            link(nc.vector.tensor_reduce(passes[0:1, 6:7], passes[0:1, 1:MAX_PASS], AX_X, ALU.add))
            link(nc.vector.tensor_scalar(passes[0:1, 7:8], passes[0:1, 6:7], 1.0, None, ALU.add))
            nc.vector.tensor_copy(passes_i, passes[0:1, 7:8]).then_inc(sem("passes_ready"), 1)
            dve.wait_ge(sem("passes_ready"), 1)

            def add_outputs():
                nc.vector.tensor_tensor(h[:, 1, 512:D], h[:, 1, 512:D], ps[:, 3, :], ALU.add).then_inc(sem("comb_read"), 1)
                nc.vector.tensor_tensor(h[0:NS, 2, :], h[0:NS, 2, :], both(4)[0:NS], ALU.add).then_inc(sem("comb_read"), 1)
                nc.vector.tensor_tensor(h[:, 1, 0:512], h[:, 1, 0:512], ps[:, 0, :], ALU.add).then_inc(sem("comb_read"), 1)
                nc.vector.tensor_tensor(h[:, 0, :], h[:, 0, :], both(6), ALU.add).then_inc(sem("comb_read"), 1)

            dve.wait_ge(sem("bias_in"), 32)
            npass = dve.value_load(passes_i, min_val=1, max_val=MAX_PASS)
            with dve.Fori(0, npass) as p:
                with dve.Fori(0, NE) as e:
                    it = p * NE + e
                    dve.wait_ge(sem("pos_shifted"), 2 * p + 2)
                    dve.wait_ge(sem("gather_ps"), it + 1)
                    dve.wait_ge(sem("GT_ps"), it + 1)
                    for i in range(3):
                        n = ROWS[i]
                        where, weight = posm[0:n, i, bass.ds(e, 1)], gate[0:n, i, bass.ds(e, 1)]
                        nc.vector.tensor_scalar(S1[0:n, i, :], const("slot", n)[:, 0:C], where, None, ALU.is_equal)
                        nc.vector.tensor_scalar(S2[0:n, i, :], const("slot", n), where, weight, ALU.is_equal, ALU.mult)
                    nc.vector.tensor_copy(sel[0:NE], ident[0:NE, bass.ds(e, 1)].broadcast_to([NE, C])).then_inc(sem("S_ready"), 1)
                    dve.wait_ge(sem("gather_ps"), it + 2)
                    nc.vector.tensor_tensor(d3(xT, C), d3(ps[:, 0, :], C), vecs[:, 8:16].unsqueeze(2).broadcast_to([P, KT, C]), ALU.mult).then_inc(sem("xT_ready"), 1)
                    dve.wait_ge(sem("expert_slot_used"), RING * it + (RING + KT))
                    hid = d3(both(1), 2)
                    nc.vector.tensor_scalar(xg, hid[:, :, 0], LIMIT, None, ALU.min).then_inc(sem("glu_ready"), 1)
                    nc.vector.tensor_scalar(xl, hid[:, :, 1], -LIMIT, LIMIT, ALU.max, ALU.min).then_inc(sem("hid_read"), 1)
                    dve.wait_ge(sem("hid_read"), it + 2)
                    nc.vector.scalar_tensor_tensor(xl, xl, 1.0, xg, ALU.add, ALU.mult).then_inc(sem("lin_glu"), 1)
                    dve.wait_ge(sem("lin_glu"), it + 1)
                    dve.wait_ge(sem("sig_ready"), it + 1)
                    nc.vector.tensor_tensor(gg, xl, sg, ALU.mult).then_inc(sem("g_ready"), 1)
                    dve.wait_ge(sem("comb_ps"), it + 1)
                    dve.wait_ge(sem("comb_read"), 4 * it + 4)
                    add_outputs()
                nc.vector.tensor_scalar(posm[:, 0:2, :], posm[:, 0:2, :], float(-C), None, ALU.add).then_inc(sem("pos_shifted"), 1)
                nc.vector.tensor_scalar(posm[0:NS, 2, :], posm[0:NS, 2, :], float(-C), None, ALU.add).then_inc(sem("pos_shifted"), 1)
            dve.wait_ge(sem("comb_ps"), npass * NE + 1)
            dve.wait_ge(sem("comb_read"), npass * (4 * NE) + 4)
            add_outputs()
            dve.wait_ge(sem("comb_read"), npass * (4 * NE) + 8)

            row_sums(2)
            row_rstd(2)
            dve.wait_ge(sem("rstd_ready"), 3)
            dve.wait_ge(sem("nfin_in"), 16)
            for i in range(3):
                n = ROWS[i]
                nc.vector.scalar_tensor_tensor(h[0:n, i, :], h[0:n, i, :], stat[0:n, 20 + i:21 + i], nfin[0:n], ALU.mult, ALU.mult).then_inc(sem("y_final"), 1)

        @block.tensor
        def _(pe):
            pe.wait_ge(sem("const_in"), 16)
            pe.wait_ge(sem("vec_in"), 16 * 8)
            pe.wait_ge(sem("rows_in"), 48)
            nc.tensor.transpose(ps[:, 7, 0:28], rows_small[0:28, 0:P], ident[0:28, 0:28])
            nc.tensor.matmul(ps[:, 7, 32:112], const("ones")[0:1, :], rows_small[0:1, P:P + 80], start=True, stop=True)
            for i in range(CT):
                last = nc.tensor.transpose(ps[:, 6, 29 * i:29 * i + 29], rows29[0:29, P * i:P * i + P], ident[0:29, 0:29])
            last.then_inc(sem("misc_ps"), 1)

            def transposed_tokens(call):
                pe.wait_ge(sem("xn_ready"), 3 * call + 3)
                for k in range(KT):
                    if k >= 2:
                        pe.wait_ge(sem("xnT_dve" if k % 2 == 0 else "xnT_act"), 4 * call + k // 2)
                    for c in range(3):
                        last = nc.tensor.transpose(ps[:, k % 2, cols(c)], xn[0:ROWS[c], c, k * P:(k + 1) * P], ident[0:ROWS[c], 0:ROWS[c]])
                    last.then_inc(sem("xnT_ps"), 1)
                pe.wait_ge(sem("xnT_dve"), 4 * call + 4)
                pe.wait_ge(sem("xnT_act"), 4 * call + 4)

            transposed_tokens(0)
            for kind, i in STEPS:
                if kind == "proj":
                    item = ("w_in", i - i % 2)
                    if i % 2 == 0:
                        mix_full(pe, item)
                    if i >= 2:
                        wait_proj_out(pe, i - 2)
                    w = d3(slot(ITEM_AT[item] % MIX_RING), 2 * P)
                    for k in range(KT):
                        last = nc.tensor.matmul(ps[:, i % 2, 0:TOK], w[:, k, (i % 2) * P:(i % 2) * P + P], xnT[:, k, :], start=(k == 0), stop=(k == KT - 1))
                    last.then_inc(sem("slot_used" if i % 2 else "proj_ps"), 1)
                elif kind == "nat":
                    n = NAT[i]
                    what, j, _ = TILES[n]
                    if what == "x":
                        pe.wait_ge(sem("silu_ready"), j + 1)
                        src = xbcT[:, j, :]
                    else:
                        wait_proj_out(pe, n)
                        src = kT[:, j, :] if what == "k" else utmp[:, UT.index(n) % 3, :]
                    if i:
                        wait_nat_out(pe, i - 1)
                    for c in range(3):
                        last = nc.tensor.transpose(ps[0:ROWS[c], 2, c * P:(c + 1) * P], src[:, cols(c)], ident)
                    last.then_inc(sem("nat_ps"), 1)
                elif kind == "ktrans":
                    for half in range(2):
                        mix_full(pe, ("k", i, half))
                        kc = d3(slot(ITEM_AT[("k", i, half)] % MIX_RING), AW)
                        for j in range(4):
                            q = 4 * half + j
                            if q >= 2:
                                pe.wait_ge(sem("ktrans_act" if q % 2 == 0 else "ktrans_dve"), 4 * i + q // 2)
                            for m in range(4):
                                last = nc.tensor.transpose(ps[:, 4 + q % 2, m * P:(m + 1) * P], kc[:, m, j * P:(j + 1) * P], ident)
                            last.then_inc(sem("ktrans_ps" if j < 3 else "slot_used"), 1)
                elif kind == "score":
                    pe.wait_ge(sem("Qz_ready"), 4)
                    pe.wait_ge(sem("ktrans_act"), 4 * i + 4)
                    pe.wait_ge(sem("ktrans_dve"), 4 * i + 4)
                    if i:
                        pe.wait_ge(sem("att_s"), i)
                    else:
                        for n in range(4, 8):
                            wait_proj_out(pe, n)
                    for half in range(2):
                        for j in range(4):
                            nc.tensor.matmul(ps[32 * j:32 * j + 32, 6 + half, :], Qz[:, i, j, :], kTb[:, j, 512 * half:512 * half + 512], start=True, stop=True)
                    for j in range(4):
                        last = nc.tensor.matmul(ps[32 * j:32 * j + 32, 3, 0:NS], Qz[:, i, j, :], kT[:, j, SEQ:TOK], start=True, stop=True)
                    last.then_inc(sem("score_ps"), 1)
                elif kind == "ptrans":
                    pe.wait_ge(sem("P_ready"), i + 1)
                    for k in range(8):
                        nc.tensor.transpose(ps[:, 4 + k // 4, (k % 4) * P:(k % 4 + 1) * P], Pb[:, i % 2, k * P:(k + 1) * P], ident)
                    nc.tensor.transpose(ps[0:NS, 3, 128:256], Pb[:, i % 2, PAST:PAST + NS], ident).then_inc(sem("ptrans_ps"), 1)
                elif kind == "pv":
                    pe.wait_ge(sem("PT_act"), i + 1)
                    pe.wait_ge(sem("PT_dve"), i + 1)
                    if i == 0:
                        for n in range(4, 8):
                            wait_nat_out(pe, n)
                    for half in range(2):
                        mix_full(pe, ("v", i, half))
                        vc = d3(slot(ITEM_AT[("v", i, half)] % MIX_RING), AW)
                        for m in range(4):
                            k = 4 * half + m
                            last = nc.tensor.matmul(ps[32 * m:32 * m + 32, 6, :], PTb[:, i % 2, k * 32:k * 32 + 32], vc[:, m, :],
                                                    start=(half == 0), stop=(half == 1 and m > 0))
                        last.then_inc(sem("slot_used"), 1)
                    nc.tensor.matmul(ps[0:32, 6, :], PTb[0:NS, i % 2, 256:288], v[0:NS, 2, :], start=False, stop=True).then_inc(sem("pv_ps"), 1)
                elif kind == "gather_o":
                    pe.wait_ge(sem("OV_ready"), i + 1)
                    nc.tensor.matmul(ps[0:NS, 3, :], const("to_token")[:, NS * i:NS * i + NS], OVm[:, i % 2, :], start=True, stop=True).then_inc(sem("go_ps"), 1)

            pe.wait_ge(sem("att_s"), DB)
            pe.wait_ge(sem("wdt_in"), 16)
            for c in range(3):
                for k in range(KT):
                    last = nc.tensor.matmul(ps[0:ROWS[c], 3, H * c:H * c + H], xnT[:, k, cols(c)], w_dt[:, k, :], start=(k == 0), stop=(k == KT - 1))
            last.then_inc(sem("dt_ps"), 1)

            wait_proj_out(pe, NT - 2)
            wait_proj_out(pe, NT - 1)

            def prompt_scores(hd):
                if hd >= 2:
                    pe.wait_ge(sem("ps_biased"), hd - 1)
                r, j = slice(64 * (hd % 2), 64 * (hd % 2) + 64), hd // 2
                nc.tensor.matmul(ps[:, 4 + hd % 2, 0:P], qT[r, j, 0:P], kT[r, j, 0:P], start=True, stop=True)
                nc.tensor.matmul(ps[:, 4 + hd % 2, P:3 * P], qT[r, j, P:2 * P], kT[r, j, 0:2 * P], start=True, stop=True).then_inc(sem("pps_ps"), 1)

            prompt_scores(0)
            for hd in range(AH):
                if hd + 1 < AH:
                    prompt_scores(hd + 1)
                pe.wait_ge(sem("pp_exp"), hd + 1)
                if hd >= 2:
                    pe.wait_ge(sem("ppT_act"), hd - 1)
                for m in range(3):
                    last = nc.tensor.transpose(ps[:, 6 + hd % 2, m * P:(m + 1) * P], Pp[:, hd % 2, m * P:(m + 1) * P], ident)
                last.then_inc(sem("ppT_ps"), 1)
                pe.wait_ge(sem("ppT_act"), hd + 1)
                c = slice(hd * AE, hd * AE + AE)
                nc.tensor.matmul(ps[:, 0, c], PTp[:, hd % 2, 0:P], v[:, 0, c], start=True, stop=True)
                nc.tensor.matmul(ps[:, 1, c], PTp[:, hd % 2, P:2 * P], v[:, 0, c], start=True, stop=False)
                last = nc.tensor.matmul(ps[:, 1, c], PTp[:, hd % 2, 2 * P:3 * P], v[:, 1, c], start=False, stop=True)
            last.then_inc(sem("pav_ps"), 1)

            pe.wait_ge(sem("ps_biased"), AH)
            for q in range(3):
                if q >= 2:
                    pe.wait_ge(sem("conv_o_dve"), q - 1)
                    pe.wait_ge(sem("conv_o_act"), q - 1)
                bank = 4 + 2 * (q % 2)
                for m in range(4):
                    last = nc.tensor.transpose(ps[0:3, bank, m * P:(m + 1) * P], xbcP[:, 4 * q + m, XS0 - 3:XS0], ident)
                last.then_inc(sem("conv_out_ps"), 1)
                for m in range(4):
                    last = nc.tensor.transpose(ps[0:DB * 7, bank + 1, m * P:(m + 1) * P], xbcP[:, 4 * q + m, XS0:XP], ident)
                last.then_inc(sem("conv_out_ps"), 1)

            dA = dts[:, 48:96]
            pe.wait_ge(sem("att_prompt_out"), 2)
            pe.wait_ge(sem("dt_ready"), 1)
            for i in range(len(NAT)):
                wait_nat_out(pe, i)
            pe.wait_ge(sem("conv_o_dve"), 3)
            pe.wait_ge(sem("conv_o_act"), 3)
            for c in range(3):
                n = ROWS[c]
                if c:
                    pe.wait_ge(sem("cs_ready"), c)
                for g in range(G):
                    nc.tensor.matmul(ps[0:n, 0, g * P:g * P + n], xbcT[:, 8 + g, cols(c)], xbcT[:, 10 + g, cols(c)], start=True, stop=True)
                nc.tensor.matmul(ps[0:n, 1, 0:H], le(c), dA[0:n, H * c:H * c + H], start=True, stop=True)
                nc.tensor.matmul(ps[0:n, 1, H:2 * H], same(c), dA[0:n, H * c:H * c + H], start=True, stop=True).then_inc(sem("gram_ps"), 1)

                def diagonal(batch):
                    pe.wait_ge(sem("M_ready"), batch + 1)
                    pe.wait_ge(sem("X_ready"), c + 1)
                    if batch % 4 == 0 and c:
                        pe.wait_ge(sem("yd_out"), c)
                    for u in range(4):
                        hd = 4 * (batch % 4) + u
                        last = nc.tensor.matmul(ps[0:n, 4 + hd // 8, (hd % 8) * HP:(hd % 8 + 1) * HP], d3(Mb[batch % 2], P)[0:n, u, 0:n],
                                                d3(Xh, HP)[0:n, hd, :], start=True, stop=True)
                    last.then_inc(sem("yd_ps"), 1)

                for hb in range(4):
                    batch = 4 * c + hb
                    pe.wait_ge(sem("dAm_ready"), batch + 1)
                    if batch >= 2:
                        pe.wait_ge(sem("L_ready"), batch - 1)
                    for u in range(4):
                        last = nc.tensor.matmul(ps[0:n, 2 + batch % 2, u * P:u * P + n], d3(dAm[batch % 2], P)[0:n, u, 0:n], le(c), start=True, stop=True)
                    last.then_inc(sem("seg_ps"), 1)
                    if hb:
                        diagonal(batch - 1)
                diagonal(4 * c + 3)

                def chunk_state():
                    pe.wait_ge(sem("Xd_ready"), c + 1)
                    for g in range(G):
                        last = nc.tensor.matmul(ps[:, 6 + g, :], Bn[:, c, g * N:(g + 1) * N], Xd[:, 512 * g:512 * g + 512], start=True, stop=True)
                    last.then_inc(sem("st_ps"), 1)

                if c == 0:
                    chunk_state()
                if c == 1:
                    pe.wait_ge(sem("St_ready"), 1)
                    for g in range(G):
                        last = nc.tensor.matmul(ps[:, 6 + g, :], xbcT[:, 10 + g, cols(c)], St[:, 512 * g:512 * g + 512], start=True, stop=True)
                    last.then_inc(sem("yo_ps"), 1)
                    pe.wait_ge(sem("yo_out"), 1)
                    chunk_state()
                    pe.wait_ge(sem("St_ready"), 2)
                    for j in range(8):
                        last = nc.tensor.transpose(ps[:, 6 + j // 4, (j % 4) * P:(j % 4 + 1) * P], St[:, j * P:(j + 1) * P], ident)
                    last.then_inc(sem("fin_ps"), 1)
            pe.wait_ge(sem("cs_ready"), 3)
            pe.wait_ge(sem("fin_ready"), 1)
            pe.wait_ge(sem("CTm_ready"), 2)
            for b in range(DB):
                pe.wait_ge(sem(f"state_in{b}"), 16)
                for j in range(8):
                    last = nc.tensor.transpose(ps[:, j // 4, (j % 4) * P:(j % 4 + 1) * P], state[:, b, j, :], ident)
                last.then_inc(sem("stT_ps"), 1)
                pe.wait_ge(sem("stT_ready"), b + 1)
                for g in range(G):
                    last = nc.tensor.matmul(ps[0:NS, 6 + g, :], CTm[g][:, NS * b:NS * b + NS], stT[:, 512 * g:512 * g + 512], start=(b == 0), stop=(b == DB - 1))
            last.then_inc(sem("yo_ps"), 1)
            pe.wait_ge(sem("dAx_ready"), 1)
            pe.wait_ge(sem("L_ready"), 12)
            for j in range(8):
                last = nc.tensor.matmul(ps[:, 2, 8 * j:8 * j + 8], dAx[0:NS, j * P:(j + 1) * P], const("seq_of", NS), start=True, stop=True)
                if j == 0:
                    last.then_inc(sem("expert_slot_used"), RING - MIX_RING)
            last.then_inc(sem("decay_ps"), 1)
            pe.wait_ge(sem("Bm_ready"), 2)
            pe.wait_ge(sem("Xd_ready"), 3)
            pe.wait_ge(sem("yd_out"), 3)
            pe.wait_ge(sem("yo_out"), 2)
            for j in range(8):
                if j >= 2:
                    pe.wait_ge(sem("state_new"), j - 1)
                for half in range(2):
                    last = nc.tensor.matmul(ps[:, 4 + 2 * (j % 2) + half, :], Xd[0:NS, j * P:(j + 1) * P],
                                            Bm[0:NS, j // 4, 4 * half:4 * half + 4, :].rearrange("p b n -> p (b n)"), start=True, stop=True)
                last.then_inc(sem("fs_ps"), 1)

            pe.wait_ge(sem("mix_ready"), 3)
            for k in range(12):
                if k >= 2:
                    pe.wait_ge(sem("mixT_dve" if k % 2 == 0 else "mixT_act"), k // 2)
                for c in range(3):
                    n = ROWS[c]
                    src = y[0:n, c, k * P:(k + 1) * P] if k < 8 else att[0:n, c, (k - 8) * P:(k - 7) * P]
                    last = nc.tensor.transpose(ps[:, k % 2, cols(c)], src, ident[0:n, 0:n])
                last.then_inc(sem("mixT_ps"), 1)
            pe.wait_ge(sem("mixT_dve"), 6)
            pe.wait_ge(sem("mixT_act"), 6)
            pe.wait_ge(sem("state_new"), 8)
            pe.wait_ge(sem("edx_ready"), 1)
            for k in range(12):
                i = k // 2
                if k % 2 == 0:
                    mix_full(pe, ("w_out", i))
                w = d3(slot(ITEM_AT[("w_out", i)] % MIX_RING), D)[:, k % 2, :]
                first, final = k == 0, k == 11
                for half in range(2):
                    for c in range(2):
                        nc.tensor.matmul(ps[:, 2 + 2 * c + half, :], mixT[:, k, cols(c)], w[:, 512 * half:512 * half + 512], start=first, stop=final)
                for half in range(2):
                    last = nc.tensor.matmul(ps[NS * half:NS * half + NS, 6, :], mixT[:, k, cols(2)], w[:, 512 * half:512 * half + 512], start=first, stop=final)
                if k == 1:
                    last.then_inc(sem("slot_used"), 1)
                if k % 2 == 1 and i >= 2:
                    last.then_inc(sem("expert_slot_used"), 2 if i == 5 else 1)

            transposed_tokens(1)
            pe.wait_ge(sem("wr_in"), 16)
            for c in range(3):
                for k in range(KT):
                    last = nc.tensor.matmul(ps[0:ROWS[c], 2, NE * c:NE * c + NE], xnT[:, k, cols(c)], w_router[:, k, :], start=(k == 0), stop=(k == KT - 1))
            last.then_inc(sem("logit_ps"), 1)
            pe.wait_ge(sem("mask_ready"), 1)
            for c in range(3):
                n = ROWS[c]
                for d in range(c):
                    nc.tensor.matmul(ps[0:n, 3, NE * c:NE * c + NE], const("ones")[:, 0:n], mask[:, d, :], start=(d == 0), stop=False)
                nc.tensor.matmul(ps[0:n, 3, NE * c:NE * c + NE], const("lt", n)[:, 0:n], mask[0:n, c, :], start=(c == 0), stop=True)
            for c in range(3):
                n = ROWS[c]
                last = nc.tensor.matmul(ps[0:1, 3, 3 * NE:4 * NE], const("ones", n)[:, 0:1], mask[0:n, c, :], start=(c == 0), stop=(c == 2))
                if c < 2:
                    last.then_inc(sem(("gather_ps", "GT_ps")[c]), 1)
            last.then_inc(sem("pos_ps"), 1)

            def combine():
                for c, banks in ((1, (0, 3)), (2, (4, 5)), (0, (6, 7))):
                    for half in range(2):
                        r = slice(C * half, C * half + C)
                        last = nc.tensor.matmul(ps[0:ROWS[c], banks[half], :], GT[r, cols(c)], ysb[r, :], start=True, stop=True)
                last.then_inc(sem("comb_ps"), 1)

            pe.wait_ge(sem("bias_in"), 32)
            pe.wait_ge(sem("passes_ready"), 1)
            npass = pe.value_load(passes_i, min_val=1, max_val=MAX_PASS)
            with pe.Fori(0, npass) as p:
                with pe.Fori(0, NE) as e:
                    it = p * NE + e
                    pe.wait_ge(sem("S_ready"), it + 1)
                    pe.wait_ge(sem("comb_read"), 4 * it + 4)
                    for k in range(KT):
                        for c in range(3):
                            n = ROWS[c]
                            last = nc.tensor.matmul(ps[:, 0, k * C:(k + 1) * C], xn[0:n, c, k * P:(k + 1) * P], S1[0:n, c, :], start=(c == 0), stop=(c == 2))
                    last.then_inc(sem("gather_ps"), 1)
                    pe.wait_ge(sem("hid_read"), it + 1)
                    for m in range(2):
                        for half in range(2):
                            nc.tensor.matmul(ps[C * half:C * half + C, 1 + m, :], sel[0:NE, :], b1s[0:NE, D * half + 512 * m:D * half + 512 * m + 512], start=True, stop=False)
                    pe.wait_ge(sem("xT_ready"), it + 1)
                    for k in range(KT):
                        s = moe_slot(k)
                        pe.wait_ge(sem(f"slot_full{s}"), 16 * it + (moe_base(s) + 16))
                        for m in range(2):
                            for half in range(2):
                                last = nc.tensor.matmul(ps[C * half:C * half + C, 1 + m, :], xT[:, k * C:(k + 1) * C],
                                                        slot(s)[:, D * half + 512 * m:D * half + 512 * m + 512], start=False, stop=(k == KT - 1))
                        last.then_inc(sem("expert_slot_used"), 1)
                    pe.wait_ge(sem("GT_ready"), it + 1)
                    pe.wait_ge(sem("ysb_ready"), it + 1)
                    combine()
                    pe.wait_ge(sem("g_ready"), it + 1)
                    pe.wait_ge(sem("comb_read"), 4 * it + 5)
                    for j in range(4):
                        last = nc.tensor.transpose(ps[:, 3, j * P:(j + 1) * P], gg[:, j * P:(j + 1) * P], ident)
                    last.then_inc(sem("gT_ps"), 1)
                    pe.wait_ge(sem("comb_read"), 4 * it + 6)
                    for half in range(2):
                        nc.tensor.matmul(ps[C * half:C * half + C, 4, :], sel[0:NE, :], b2s[0:NE, 512 * half:512 * half + 512], start=True, stop=False)
                    for c in range(3):
                        n = ROWS[c]
                        last = nc.tensor.transpose(ps[:, 5, cols(c)], S2[0:n, c, :], ident[0:n, 0:n])
                    last.then_inc(sem("GT_ps"), 1)
                    pe.wait_ge(sem("gT_ready"), it + 1)
                    for k in range(KT):
                        s = moe_slot(KT + k // 2)
                        if k % 2 == 0:
                            pe.wait_ge(sem(f"slot_full{s}"), 16 * it + (moe_base(s) + 16))
                        for half in range(2):
                            last = nc.tensor.matmul(ps[C * half:C * half + C, 4, :], gT[:, (k % 4) * P + C * (k // 4):(k % 4) * P + C * (k // 4) + C],
                                                    slot(s)[:, D * (k % 2) + 512 * half:D * (k % 2) + 512 * half + 512], start=False, stop=(k == KT - 1))
                        if k % 2 == 1:
                            last.then_inc(sem("expert_slot_used"), 1)
            pe.wait_ge(sem("GT_ready"), npass * NE + 1)
            pe.wait_ge(sem("ysb_ready"), npass * NE + 1)
            pe.wait_ge(sem("comb_read"), npass * (4 * NE) + 4)
            combine()


INPUTS = ["x_prompt", "x_sample", "state_conv", "state_ssm", "cache_win_k", "cache_win_v", "norm_mix", "w_in", "conv_w", "conv_b",
          "dt_bias", "a_log", "d_skip", "ssd_norm", "att_norm", "w_out", "norm_ffn", "router_w", "router_b", "w1", "b1", "w2", "b2", "norm_final"]
OUTPUTS = [("y_prompt", (SEQ, D), (1, SEQ, D)), ("y_sample", (NS, D), (DB, DT, D)),
           ("conv_prompt", (3, CD), (1, 1, 3, CD)), ("ssm_prompt", (H, HP, N), (1, 1, H, HP, N)),
           ("k_prompt", (SEQ, AH, AE), (1, 1, SEQ, AH, AE)), ("v_prompt", (SEQ, AH, AE), (1, 1, SEQ, AH, AE)),
           ("conv_sample", (DB, 3, CD), (1, DB, 3, CD)), ("ssm_sample", (DB, H, HP, N), (1, DB, H, HP, N)),
           ("k_sample", (NS, AH, AE), (1, DB, DT, AH, AE)), ("v_sample", (NS, AH, AE), (1, DB, DT, AH, AE))]


def kernel(**inputs):
    from concourse import bacc
    from concourse.bass_utils import run_bass_kernel_spmd

    nc = bacc.Bacc("TRN2", target_bir_lowering=False, num_devices=1)
    arrays = {name: np.ascontiguousarray(inputs[name]) for name in INPUTS}
    arrays |= {"consts": CONSTS, "bias_old": BIAS_OLD, "bias_prompt": BIAS_PROMPT}
    a = {n: nc.dram_tensor("in_" + n, v.shape, mybir.dt.from_np(v.dtype), kind="ExternalInput").ap() for n, v in arrays.items()}
    o = {n: nc.dram_tensor("out_" + n, shape, F32, kind="ExternalOutput").ap() for n, shape, _ in OUTPUTS}
    hymba_step(nc, a, o)
    r = run_bass_kernel_spmd(nc, [{"in_" + n: v for n, v in arrays.items()}], core_ids=[0])
    return tuple(r.results[0]["out_" + n].reshape(full) for n, _, full in OUTPUTS)
```

```python
from contextlib import ExitStack

import numpy as np

import concourse.bass as bass
from concourse import mybir

F32 = mybir.dt.float32
BF16 = mybir.dt.bfloat16
I32 = mybir.dt.int32
U32 = mybir.dt.uint32
ALU = mybir.AluOpType
ACT = mybir.ActivationFunctionType
AX_X = mybir.AxisListType.X

P = 128
D = 1024
KT = D // P
SEQ = 256
DB, DT = 8, 4
NS = DB * DT
TOK = SEQ + NS
ROWS = [P, P, NS]
PAST = 1024
H, HP, N = 16, 64, 128
SSD = H * HP
G = 2
CONV = 4
CD = SSD + 2 * G * N
CT = CD // P
AH, AE = 8, 64
AW = AH * AE
MIX = SSD + AW
IN_W = SSD + CD + H + 3 * AW
NE, TOPK = 32, 4
PAIRS = NE // 2
F2 = 2 * D
LIMIT, ALPHA, EPS = 7.0, 1.702, 1e-5
PATTERNS = ((128, 1), (512, 4), (2048, 16))
NEG = -1e30

C = 64
MAX_PASS = -(-TOK // C)
SLOT = 2048
RING = 12
MIX_RING = 5

Z0, X0, B0_, C0_ = 0, SSD, 2 * SSD, 2 * SSD + G * N
DT0 = SSD + CD
Q0 = DT0 + H
K0, V0 = Q0 + AW, Q0 + 2 * AW
TILES = ([("q", i, Q0 + i * P) for i in range(4)] + [("k", i, K0 + i * P) for i in range(4)]
         + [("v", i, V0 + i * P) for i in range(4)] + [("x", i, X0 + i * P) for i in range(CT)]
         + [("z", i, Z0 + i * P) for i in range(8)])
NT = len(TILES)
NAT = [n for n, (kind, i, _) in enumerate(TILES) if kind in "kvz" or (kind == "x" and i < 10)]

XP = 3 + SEQ + DB * (3 + DT)
XS0 = 3 + SEQ
XC = XP - 3


def shape_constants():
    parts, at, pos = [], {}, 0

    def put(name, a):
        nonlocal pos
        a = np.asarray(a, np.float32)
        full = np.zeros((P, a.shape[1]), np.float32)
        full[:a.shape[0]] = a
        parts.append(full)
        at[name] = (pos, a.shape[1])
        pos += a.shape[1]

    r = np.arange(P)
    put("ident", np.eye(P))
    put("le", r[:, None] <= r[None, :])
    put("gt", r[:, None] > r[None, :])
    put("lt", r[:, None] < r[None, :])
    put("ones", np.ones((P, P)))
    put("slot", np.tile(r % C, (P, 1)))
    s = np.arange(NS)
    same = (s[:, None] // DT) == (s[None, :] // DT)
    put("le_s", (s[:, None] <= s[None, :]) & same)
    put("gt_s", (s[:, None] > s[None, :]) & same)
    put("same_s", same)
    put("expert", np.tile(np.arange(NE), (P, 1)))
    put("expert_row", (r[:96, None] % NE) == np.arange(NE + 2)[None, :])
    put("seq_of", (s[:, None] // DT) == np.arange(DB)[None, :])
    put("half", (r[:, None] // HP) == np.arange(2)[None, :])
    put("seq_cols", np.tile(((s[None, :] // DT) == np.arange(DB)[:, None]).reshape(1, -1), (P, 1)))
    row_h, row_t = (r % 32) // DT, r % DT
    put("head_of", row_h[:, None] == np.arange(AH)[None, :])
    tok = np.arange(NS)
    put("to_token", (tok[None, None, :] == DT * np.arange(DB)[None, :, None] + row_t[:, None, None])
        .reshape(P, -1))
    slopes = 2.0 ** (-8.0 * np.arange(1, AH + 1) / AH)

    def bias(h, d):
        count = sum(((d >= 0) & (d % dil == 0) & (d // dil <= w // dil)).astype(np.float64)
                    for w, dil in PATTERNS)
        return np.where(count > 0, -slopes[h] * d + np.log(np.maximum(count, 1)), NEG)

    used = (r % 32) < 2 * DT
    h_row = np.minimum(2 * (r // 32) + (r % 32) // DT, AH - 1)
    t_row = r % DT
    d_new = t_row[:, None, None] - (tok[None, None, :] % DT) + 0 * np.arange(DB)[None, :, None]
    own = (tok[None, None, :] // DT) == np.arange(DB)[None, :, None]
    new = np.where(own & (d_new >= 0), bias(h_row[:, None, None], d_new), NEG)
    put("bias_new", np.where(used[:, None, None], new, 0).reshape(P, -1))
    consts = np.concatenate(parts, 1)
    d_old = PAST + t_row[:, None] - np.arange(PAST)[None, :]
    bias_old = np.where(used[:, None], bias(h_row[:, None], d_old), 0).astype(np.float32)
    d_prompt = r[:, None, None] + P - np.arange(2 * P)[None, None, :] + 0 * np.arange(AH)[None, :, None]
    bias_prompt = bias(np.arange(AH)[None, :, None], d_prompt).astype(np.float32).reshape(P, -1)
    return consts, at, bias_old, bias_prompt


CONSTS, CONST_AT, BIAS_OLD, BIAS_PROMPT = shape_constants()


def mixer_steps():
    steps, nat = [], 0

    def proj(n):
        steps.append(("proj", n))

    def back(last):
        nonlocal nat
        if nat < len(NAT) and NAT[nat] <= last:
            steps.append(("nat", nat))
            nat += 1

    for n in range(12):
        proj(n)
        back(n - 2)
    steps.append(("ktrans", 0))
    for b in range(DB):
        steps.append(("score", b))
        if b:
            steps.append(("gather_o", b - 1))
        proj(12 + 2 * b)
        back(10 + 2 * b)
        if b + 1 < DB:
            steps.append(("ktrans", b + 1))
            back(10 + 2 * b)
        convs = [i for i in (2 * b - 1, 2 * b) if 0 <= i < CT]
        steps.extend(("conv", i) for i in convs)
        steps.append(("ptrans", b))
        steps.extend(("silu", i) for i in convs)
        proj(13 + 2 * b)
        back(11 + 2 * b)
        steps.append(("pv", b))
    back(26)
    steps.append(("gather_o", DB - 1))
    steps.append(("dt", 0))
    steps.extend(("conv_out", q) for q in range(3))
    steps.extend([("p_score", 0), ("p_score", 1)])
    for hd in range(AH):
        steps.append(("p_trans", hd))
        if hd % 2 == 0:
            proj(28 + hd // 2)
            back(26 + hd // 2)
        else:
            back(NT - 4)
            back(NT - 4)
        steps.append(("p_out", hd))
        if hd + 2 < AH:
            steps.append(("p_score", hd + 2))
    while nat < len(NAT):
        back(NT)
    return steps


STEPS = mixer_steps()
NAT_ON_DVE = [i for i in range(len(NAT)) if i < 8 and i % 2 == 0]
NAT_ON_ACT = [i for i in range(len(NAT)) if i not in NAT_ON_DVE]


def ring_items():
    items = []
    for kind, i in STEPS:
        if kind == "proj" and i % 2 == 1:
            items.append(("w_in", i - 1))
        if kind == "ktrans":
            items += [("k", i, 0), ("k", i, 1)]
        if kind == "pv":
            items += [("v", i, 0), ("v", i, 1)]
    return items + [("w_out", i) for i in range(MIX // P // 2)]


ITEMS = ring_items()
ITEM_AT = {item: n for n, item in enumerate(ITEMS)}


def hymba_step(nc, a, o):
    ctx = ExitStack()
    with ctx:
        sems = {}

        def sem(name):
            if name not in sems:
                sems[name] = ctx.enter_context(nc.semaphore(name))
            return sems[name]

        ring = ctx.enter_context(nc.sbuf_tensor("ring", [P, RING * SLOT], F32))
        WORDS = 28500
        own = ctx.enter_context(nc.sbuf_tensor("own", [P, WORDS], F32))
        ps = ctx.enter_context(nc.psum_tensor("ps", [P, 8, 512], F32))

        used = [0]

        def take(words):
            used[0] += words
            assert used[0] <= WORDS, used[0]
            return own[:, used[0] - words:used[0]]

        def sub(region, start, words):
            return region[:, start:start + words]

        def d3(ap, b):
            return ap.rearrange("p (a b) -> p a b", b=b)

        def d4(ap, b, c):
            return ap.rearrange("p (a b c) -> p a b c", b=b, c=c)

        consts = take(CONSTS.shape[1])

        def const(name, rows=P):
            start, n = CONST_AT[name]
            return consts[0:rows, start:start + n]

        ident = const("ident")
        h = d3(take(3 * D), D)
        r_xn = take(3 * D)
        xn = d3(r_xn, D)
        xs = xn
        r_xnT = take(KT * TOK)
        xnT = d3(r_xnT, TOK)
        r_xbcP = take(CT * XP)
        xbcP = d3(r_xbcP, XP)
        y = d3(sub(r_xbcP, 0, 3 * SSD), SSD)
        r_xbcT = take(CT * TOK)
        xbcT = d3(r_xbcT, TOK)
        mixT = d3(r_xbcT, TOK)
        r_qk = take(2 * 4 * TOK)
        qT = d3(sub(r_qk, 0, 4 * TOK), TOK)
        kT = d3(sub(r_qk, 4 * TOK, 4 * TOK), TOK)
        r_z = take(3 * SSD)
        z = d3(r_z, SSD)
        r_v = take(3 * AW)
        v = d3(r_v, AW)
        r_o = take(3 * AW)
        att = d3(r_o, AW)
        Bn = d3(take(3 * G * N), G * N)
        cw = d3(take(CT * 29), 29)
        w_dt = d3(take(KT * H), H)
        w_router = d3(take(KT * NE), NE)
        vecs = take(28)
        bvec = take(80)
        stat = take(64)
        st4 = take(32)
        dts = take(6 * 48)
        r_small = take(160)
        rows_small = take(128 + 80)

        work = ring[:, MIX_RING * SLOT:RING * SLOT]
        wk = [0]

        def work_take(words):
            wk[0] += words
            assert wk[0] <= (RING - MIX_RING) * SLOT
            return work[:, wk[0] - words:wk[0]]

        r_kTb = work_take(4 * PAST)
        kTb = d3(r_kTb, PAST)
        k_nat = d3(sub(r_kTb, 0, 3 * AW), AW)
        r_Qz = work_take(DB * 4 * 32)
        Qz = r_Qz.rearrange("p (b j c) -> p b j c", b=DB, j=4)
        r_PT = work_take(2 * 288)
        PTb = d3(r_PT, 288)
        r_OV = work_take(2 * 512)
        OVm = d3(r_OV, 512)
        conv_t = d3(work_take(2 * XC), XC)
        bias_o = work_take(PAST)
        r_Pb = work_take(2 * 1056)
        Pb = d3(r_Pb, 1056)
        rows29 = r_Pb[:, 0:CD]
        bias_p = d3(work_take(AH * 2 * P), 2 * P)
        utmp = d3(work_take(3 * TOK), TOK)
        PTp = d3(work_take(768), 384)
        Pp = d3(sub(r_Pb, 0, 768), 384)
        conv_o = work[:, 4 * PAST + 1024 + 576:4 * PAST + 1024 + 576 + CD]
        conv_o_s, conv_o3 = conv_o[0:DB * 7], conv_o[64:67]

        state = work[:, 0:DB * 8 * N].rearrange("p (b j n) -> p b j n", b=DB, j=8)
        w0 = DB * 8 * N
        stT = work[:, w0:w0 + SSD]
        tmp1 = work[:, w0 + SSD:w0 + 2 * SSD]
        Xh = work[:, w0 + 2 * SSD:w0 + 3 * SSD]
        Xd = work[:, w0 + 3 * SSD:w0 + 4 * SSD]
        dAm = [work[:, w0 + 4 * SSD + i * 512:w0 + 4 * SSD + (i + 1) * 512] for i in range(2)]
        Lb = [work[:, w0 + 4 * SSD + (2 + i) * 512:w0 + 4 * SSD + (3 + i) * 512] for i in range(2)]
        Mb = [sub(r_qk, i * 512, 512) for i in range(2)]
        dAx = sub(r_qk, 1024, SSD)
        fin_nat = dAx
        Bm = r_xnT[:, 0:G * DB * N].rearrange("p (g b n) -> p g b n", g=G, b=DB)
        St = sub(r_v, 0, SSD)
        GM = sub(r_v, SSD, 2 * P)
        CTm = [sub(r_xnT, G * DB * N, DB * NS), sub(r_v, SSD + 2 * P, DB * NS)]
        ex = r_small[:, 0:48]
        edx = r_small[:, 48:112]
        cst = r_small[:, 112:144]

        xT = sub(r_xbcP, 0, 512)
        S1 = d3(sub(r_xbcP, 512, 3 * 2 * C), 2 * C)
        S2 = d3(sub(r_xbcP, 896, 3 * 2 * C), 2 * C)
        sel = d3(sub(r_xbcP, 1280, C).bitcast(BF16), C)
        GT = sub(r_xbcP, 1344, TOK)
        xg, xl, sg, gg = (sub(r_xbcP, 1632 + i * 512, 512) for i in range(4))
        gT = sub(r_v, 0, 512)
        ysb = sub(r_v, 512, D)
        b1p = sub(r_z, 0, F2 // 2).bitcast(BF16)
        b1s = sub(r_z, F2 // 2, F2)
        b1_rest = sub(r_xbcP, 0, F2)
        b1_mid = sub(r_xbcP, F2, F2 // 2).bitcast(BF16)
        nfin = sub(r_o, 0, D)
        rt = sub(r_qk, 0, 2304)
        posm = d3(sub(rt, 600, 3 * (NE + 2)), NE + 2)
        gate = d3(sub(rt, 710, 3 * (NE + 2)), NE + 2)
        mask = d3(sub(rt, 192, 96), 32)
        logit = d3(sub(rt, 288, 96), 32)
        top8 = d3(sub(rt, 384, 24), 8)
        idx8 = d3(sub(rt, 408, 24), 8)
        idxf = d3(sub(rt, 432, 24), 8)
        e4 = d3(sub(rt, 456, 12), 4)
        rs1 = sub(rt, 468, 3)
        eq1 = sub(rt, 480, 32)
        passes = sub(rt, 512, 8)
        passes_i = rt[0:1, 520:521].bitcast(I32)

        def le(c):
            return const("le") if c < 2 else const("le_s", NS)

        def gt(c):
            return const("gt") if c < 2 else const("gt_s", NS)

        def same(c):
            return const("ones") if c < 2 else const("same_s", NS)

        def cols(c):
            return slice(P * c, P * c + ROWS[c])

        def stat2(hd, which):
            return st4[:, 8 * which + hd:8 * which + hd + 1]

        block = ctx.enter_context(nc.Block())

        def slot(n):
            return ring[:, n * SLOT:(n + 1) * SLOT]

        def mix_full(eng, item):
            n = ITEM_AT[item]
            eng.wait_ge(sem(f"slot_full{n % MIX_RING}"), 16 * (n // MIX_RING + 1))

        MIX_LOADS = [len([n for n in range(len(ITEMS)) if n % MIX_RING == s]) for s in range(MIX_RING)]

        def moe_slot(j):
            return (MIX_RING + j) % RING

        def moe_base(s):
            return 16 * MIX_LOADS[s] if s < MIX_RING else 0

        def wait_proj_out(eng, n):
            if n % 2 == 0:
                eng.wait_ge(sem("proj_out_act"), n // 2 + 1)
            else:
                eng.wait_ge(sem("proj_out_dve"), n // 2 + 1)

        def wait_nat_out(eng, i):
            if i in NAT_ON_DVE:
                eng.wait_ge(sem("nat_out_dve"), NAT_ON_DVE.index(i) + 1)
            else:
                eng.wait_ge(sem("nat_out_act"), NAT_ON_ACT.index(i) + 1)

        UT = [n for n in NAT if TILES[n][0] in "vz"]

        zeroed = sem("zeroed")

        @block.sync
        def _(sp):
            sp.dma_start(h[:, 0:2, :], a["x_prompt"][0].rearrange("(i p) d -> p i d", p=P)).then_inc(sem("x_in"), 16)
            sp.dma_start(h[0:NS, 2, :], a["x_sample"].rearrange("b t d -> (b t) d")).then_inc(sem("x_in"), 16)
            sp.dma_start(consts, a["consts"]).then_inc(sem("const_in"), 16)
            sp.wait_ge(sem("vec_in"), 16 * 8)
            w_in = a["w_in"][0].rearrange("(k p) c -> p k c", p=P)
            w_out = a["w_out"][0].rearrange("(k p) c -> p k c", p=P)
            for n, item in enumerate(ITEMS):
                s = n % MIX_RING
                if item == ("w_out", 0):
                    sp.wait_ge(sem("go_ps"), DB)
                    for b in range(DB):
                        if b == 5:
                            sp.wait_ge(sem("conv_o_act"), 3)
                            sp.wait_ge(sem("conv_o_dve"), 3)
                            sp.dma_start(o["conv_prompt"], conv_o3).then_inc(sem("conv_out"), 16)
                            for q in range(DB):
                                sp.dma_start(o["conv_sample"][q], conv_o_s[7 * q + 4:7 * q + 7, :]).then_inc(sem("conv_out"), 16)
                            sp.wait_ge(sem("conv_out"), 16 * (DB + 1))
                        sp.dma_start(state[:, b], a["state_ssm"][0, b].rearrange("(j h) p n -> (h p) j n", j=8)).then_inc(sem(f"state_in{b}"), 16)
                if item == ("w_out", MIX_RING):
                    new_state = o["ssm_sample"].rearrange("b (j h) p n -> (h p) b j n", j=8)
                    for j in range(8):
                        sp.wait_ge(sem("state_new"), j + 1)
                        sp.dma_start(new_state[:, :, j, :], state[:, :, j, :]).then_inc(sem("ssm_s_out"), 16)
                if n >= MIX_RING:
                    sp.wait_ge(sem("slot_used"), n - MIX_RING + 1)
                if item[0] == "w_in":
                    c0 = TILES[item[1]][2]
                    dst, src = d3(slot(s), 2 * P), w_in[:, :, c0:c0 + 2 * P]
                elif item[0] == "w_out":
                    dst, src = d3(slot(s), D), w_out[:, 2 * item[1]:2 * item[1] + 2, :]
                else:
                    cache = a["cache_win_k" if item[0] == "k" else "cache_win_v"][0, item[1]]
                    src = cache.rearrange("(k p) h e -> p k (h e)", p=P)[:, 4 * item[2]:4 * item[2] + 4, :]
                    dst = d3(slot(s), AW)
                sp.dma_start(dst, src).then_inc(sem(f"slot_full{s}"), 16)
            sp.wait_ge(sem("work_free"), 1)
            sp.wait_ge(sem("ssm_s_out"), 16 * 8)
            w1 = a["w1"][0].rearrange("e (k p) c -> e k p c", p=P)
            w2 = a["w2"][0].rearrange("e (k p) c -> e p k c", p=P)

            def expert_loads(e, it):
                for j in range(RING):
                    s = moe_slot(j)
                    sp.wait_ge(sem("expert_slot_used"), it * RING + (j + 1))
                    if j < KT:
                        dst, src = slot(s), w1[bass.ds(e, 1), j].rearrange("e p c -> p (e c)")
                    else:
                        k2 = 2 * (j - KT)
                        dst, src = d3(slot(s), D), w2[bass.ds(e, 1), :, k2:k2 + 2].rearrange("e p k c -> p (e k) c")
                    sp.dma_start(dst, src).then_inc(sem(f"slot_full{s}"), 16)

            expert_loads(0, 0)
            with sp.Fori(1, NE) as e:
                expert_loads(e, e)
            sp.wait_ge(sem("passes_ready"), 1)
            npass = sp.value_load(passes_i, min_val=1, max_val=MAX_PASS)
            with sp.If(npass > 1):
                with sp.Fori(1, npass) as p:
                    with sp.Fori(0, NE) as e:
                        expert_loads(e, p * NE + e)

        @block.gpsimd
        def _(pool):
            nc.gpsimd.memset(xbcP[:, :, 0:3], 0.0).then_inc(zeroed, 1)
            nc.gpsimd.memset(dts, 0.0).then_inc(zeroed, 1)
            nc.gpsimd.memset(stat[:, 0:24], 1.0).then_inc(zeroed, 1)
            nc.gpsimd.memset(r_Qz, 0.0).then_inc(zeroed, 1)

            for name, src, i0 in (("k", k_nat, 0), ("v", v, 4)):
                for i in range(i0, i0 + 4):
                    wait_nat_out(pool, i)
                pool.dma_start(o[name + "_prompt"].rearrange("(i p) h e -> p i (h e)", p=P), src[:, 0:2, :]).then_inc(sem(name + "_out"), 16)
                pool.dma_start(o[name + "_sample"].rearrange("t h e -> t (h e)"), src[0:NS, 2, :]).then_inc(sem(name + "_out"), 16)

            pool.wait_ge(sem("att_prompt_out"), 2)
            dA = dts[:, 48:96]
            dt = dts[:, 0:48]
            pool.wait_ge(sem("dt_ready"), 1)
            for i in range(8, len(NAT)):
                wait_nat_out(pool, i)
            batch = 0
            for c in range(3):
                n = ROWS[c]
                x3 = d3(xs[0:n, c, :], HP)
                if c >= 1:
                    pool.wait_ge(sem("st_ps"), c)
                nc.gpsimd.tensor_tensor(d3(Xh[0:n], HP), x3, dt[0:n, 16 * c:16 * c + 16].unsqueeze(2).broadcast_to([n, H, HP]),
                                        ALU.mult).then_inc(sem("X_ready"), 1)
                nc.gpsimd.tensor_tensor(d3(y[0:n, c, :], HP), x3, bvec[0:n, 32:48].unsqueeze(2).broadcast_to([n, H, HP]),
                                        ALU.mult).then_inc(sem("DX_ready"), 1)
                for hb in range(4):
                    if batch >= 2:
                        pool.wait_ge(sem("seg_ps"), batch - 1)
                    nc.gpsimd.tensor_tensor(
                        dAm[batch % 2].rearrange("p (h s) -> p h s", h=4)[0:n, :, 0:n],
                        gt(c).unsqueeze(1).broadcast_to([n, 4, n]),
                        dA[0:n, 16 * c + 4 * hb:16 * c + 4 * hb + 4].unsqueeze(2).broadcast_to([n, 4, n]),
                        ALU.mult).then_inc(sem("dAm_ready"), 1)
                    batch += 1
                pool.wait_ge(sem("X_ready"), c + 1)
                pool.wait_ge(sem("ex_ready"), c + 1)
                nc.gpsimd.tensor_tensor(d3(Xd[0:n], HP), d3(Xh[0:n], HP), ex[0:n, 0:16].unsqueeze(2).broadcast_to([n, H, HP]),
                                        ALU.mult).then_inc(sem("Xd_ready"), 1)
            for g in range(G):
                nc.gpsimd.tensor_tensor(Bm[0:NS, g], Bn[0:NS, 2, g * N:(g + 1) * N].unsqueeze(1).broadcast_to([NS, DB, N]),
                                        const("seq_of", NS).unsqueeze(2).broadcast_to([NS, DB, N]), ALU.mult).then_inc(sem("Bm_ready"), 1)
            for g in range(G):
                nc.gpsimd.tensor_tensor(d3(CTm[g], NS), xbcT[:, 10 + g, SEQ:TOK].unsqueeze(1).broadcast_to([P, DB, NS]),
                                        d3(const("seq_cols"), NS), ALU.mult).then_inc(sem("CTm_ready"), 1)
            pool.wait_ge(sem("fin_out"), 16)
            nc.gpsimd.tensor_copy(d3(dAx[0:NS], HP), dA[0:NS, 32:48].unsqueeze(2).broadcast_to([NS, H, HP])).then_inc(sem("dAx_ready"), 1)
            pool.wait_ge(sem("mixT_ps"), 12)
            nc.gpsimd.memset(ysb, 0.0).then_inc(sem("ysb_ready"), 1)
            nc.gpsimd.memset(rt[:, 600:820], 0.0).then_inc(zeroed, 1)
            for part in range(3):
                pool.dma_start(b1s[NE * part:NE * part + NE, :], a["b1"][0]).then_inc(sem("b1_in"), 16)
            pool.wait_ge(sem("ysb_ready"), 1)
            pool.dma_start(ysb[0:NE, :], a["b2"][0]).then_inc(sem("b2_in"), 16)
            pool.dma_start(nfin, a["norm_final"].partition_broadcast(P)).then_inc(sem("nfin_in"), 16)
            pool.wait_ge(sem("b1_in"), 48)
            b1_parts = sem("b1_parts")
            nc.gpsimd.tensor_copy(b1p[0:96], b1s[0:96]).then_inc(b1_parts, 1)
            pool.wait_ge(b1_parts, 1)
            nc.gpsimd.tensor_tensor(b1_rest[0:96], b1s[0:96], b1p[0:96], ALU.subtract).then_inc(b1_parts, 1)
            pool.wait_ge(b1_parts, 2)
            nc.gpsimd.tensor_copy(b1_mid[0:96], b1_rest[0:96]).then_inc(b1_parts, 1)
            pool.wait_ge(b1_parts, 3)
            nc.gpsimd.tensor_tensor(b1s[64:96], b1_rest[64:96], b1_mid[64:96], ALU.subtract).then_inc(b1_parts, 1)
            nc.gpsimd.tensor_copy(b1p[32:64], b1_mid[32:64]).then_inc(b1_parts, 1)
            pool.wait_ge(b1_parts, 5)
            nc.gpsimd.tensor_copy(b1p[64:96], b1s[64:96]).then_inc(b1_parts, 1)
            pool.wait_ge(b1_parts, 6)
            nc.gpsimd.memset(GT, 0.0).then_inc(sem("moe_free"), 1)
            pool.wait_ge(sem("y_final"), 2)
            pool.dma_start(o["y_prompt"].rearrange("(i p) d -> p i d", p=P), h[:, 0:2, :]).then_inc(sem("y_out"), 16)
            pool.wait_ge(sem("y_final"), 3)
            pool.dma_start(o["y_sample"], h[0:NS, 2, :]).then_inc(sem("y_out"), 16)
            pool.wait_ge(sem("y_out"), 32)
            pool.wait_ge(sem("k_out"), 32)
            pool.wait_ge(sem("v_out"), 32)
            pool.wait_ge(sem("conv_out"), 16 * (DB + 1))
            pool.wait_ge(sem("fin_out"), 16)
            pool.wait_ge(sem("ssm_s_out"), 16 * 8)

        @block.scalar
        def _(act):
            act.dma_start(rows_small[0:8, 0:P], a["norm_mix"][0].rearrange("(k p) -> k p", p=P)).then_inc(sem("vec_in"), 16)
            act.dma_start(rows_small[8:16, 0:P], a["norm_ffn"][0].rearrange("(k p) -> k p", p=P)).then_inc(sem("vec_in"), 16)
            act.dma_start(rows_small[16:24, 0:P], a["ssd_norm"][0].rearrange("(k p) -> k p", p=P)).then_inc(sem("vec_in"), 16)
            act.dma_start(rows_small[24:28, 0:P], a["att_norm"][0].rearrange("(k p) -> k p", p=P)).then_inc(sem("vec_in"), 16)
            for i, name in enumerate(("dt_bias", "a_log", "d_skip")):
                act.dma_start(rows_small[0:1, P + 16 * i:P + 16 * i + 16], a[name]).then_inc(sem("vec_in"), 16)
            act.dma_start(rows_small[0:1, P + 48:P + 80], a["router_b"]).then_inc(sem("vec_in"), 16)
            act.dma_start(rows29[0:24, :], a["state_conv"][0].rearrange("b t c -> (b t) c")).then_inc(sem("rows_in"), 16)
            act.dma_start(rows29[24:28, :], a["conv_w"][0]).then_inc(sem("rows_in"), 16)
            act.dma_start(rows29[28:29, :], a["conv_b"]).then_inc(sem("rows_in"), 16)
            act.dma_start(w_dt, a["w_in"][0].rearrange("(k p) c -> p k c", p=P)[:, :, DT0:DT0 + H]).then_inc(sem("wdt_in"), 16)
            act.dma_start(w_router, a["router_w"][0].rearrange("(k p) c -> p k c", p=P)).then_inc(sem("wr_in"), 16)

            def norm_rows(first):
                act.wait_ge(sem("ss_ready"), 3 * first + 3)
                nc.scalar.activation(stat[:, 16:19], stat[:, 0:3], ACT.Sqrt).then_inc(sem("rt_ready"), 1)
                act.wait_ge(sem("rstd_ready"), first + 1)
                for i in range(3):
                    n = ROWS[i]
                    nc.scalar.activation(xn[0:n, i, :], h[0:n, i, :], ACT.Copy, scale=stat[0:n, 20 + i:21 + i]).then_inc(sem("xn_ready"), 1)

            def xT_evac(first, g0):
                for k in range(1, KT, 2):
                    act.wait_ge(sem("xnT_ps"), first * KT + k + 1)
                    nc.scalar.activation(xnT[:, k, :], ps[:, k % 2, 0:TOK], ACT.Copy, scale=vecs[:, g0 + k:g0 + k + 1]).then_inc(sem("xnT_act"), 1)

            norm_rows(0)
            act.wait_ge(sem("vec_ready"), 1)
            xT_evac(0, 0)
            act.dma_start(bias_o, a["bias_old"]).then_inc(sem("bias_o_in"), 16)
            act.dma_start(bias_p, a["bias_prompt"].rearrange("p (h k) -> p h k", h=AH)).then_inc(sem("bias_p_in"), 16)
            act.wait_ge(sem("bvec_ready"), 1)
            nc.scalar.activation(bvec[:, 16:32], bvec[:, 16:32], ACT.Exp).then_inc(sem("ea_ready"), 1)
            for kind, i in STEPS:
                if kind == "proj" and i % 2 == 0:
                    what, j, _ = TILES[i]
                    act.wait_ge(sem("proj_ps"), i // 2 + 1)
                    src = ps[:, i % 2, 0:TOK]
                    if what == "q":
                        nc.scalar.activation(qT[:, j, :], src, ACT.Copy, scale=AE ** -0.5).then_inc(sem("proj_out_act"), 1)
                    elif what == "k":
                        nc.scalar.activation(kT[:, j, :], src, ACT.Copy).then_inc(sem("proj_out_act"), 1)
                    elif what == "x":
                        nc.scalar.activation(xbcP[:, j, 3:XS0], src[:, 0:SEQ], ACT.Copy)
                        nc.scalar.activation(d3(xbcP[:, j, XS0:XP], 7)[:, :, 3:7], d3(src[:, SEQ:TOK], DT), ACT.Copy).then_inc(sem("proj_out_act"), 1)
                    else:
                        u = UT.index(i)
                        if u >= 3:
                            act.wait_ge(sem("nat_ps"), NAT.index(UT[u - 3]) + 1)
                        nc.scalar.activation(utmp[:, u % 3, :], src, ACT.Copy).then_inc(sem("proj_out_act"), 1)
                elif kind == "silu":
                    act.wait_ge(sem("conv_ready"), i + 1)
                    src = conv_t[:, i % 2, :]
                    nc.scalar.activation(xbcT[:, i, 0:SEQ], src[:, 0:SEQ], ACT.Silu)
                    nc.scalar.activation(d3(xbcT[:, i, SEQ:TOK], DT), d3(src[:, SEQ:XC], 7)[:, :, 3:7], ACT.Silu).then_inc(sem("silu_ready"), 1)
                elif kind == "nat" and i in NAT_ON_ACT:
                    what, j, _ = TILES[NAT[i]]
                    act.wait_ge(sem("nat_ps"), i + 1)
                    func = ACT.Silu if what == "z" else ACT.Copy
                    dst, j = {"k": (k_nat, j), "v": (v, j), "z": (z, j), "x": (xs, j)}[what]
                    if what == "x" and j >= 8:
                        dst, j = Bn, j - 8
                    nc.scalar.activation(dst[:, 0:2, j * P:(j + 1) * P], d3(ps[:, 2, 0:2 * P], P), func)
                    nc.scalar.activation(dst[0:NS, 2, j * P:(j + 1) * P], ps[0:NS, 2, 2 * P:3 * P], func).then_inc(sem("nat_out_act"), 1)
                elif kind == "ktrans":
                    if i == 0:
                        act.wait_ge(sem("k_out"), 32)
                    for q in range(0, 8, 2):
                        half, j = q // 4, q % 4
                        act.wait_ge(sem("ktrans_ps"), 6 * i + 3 * half + j + 1)
                        nc.scalar.activation(kTb[:, j, 512 * half:512 * half + 512], ps[:, 4 + q % 4, :], ACT.Copy).then_inc(sem("ktrans_act"), 1)
                elif kind == "score":
                    act.wait_ge(sem("score_biased"), i + 1)
                    nc.scalar.activation(Pb[:, i % 2, :], Pb[:, i % 2, :], ACT.Exp, bias=stat[:, 32 + i:33 + i],
                                         accum_out=stat[:, 40 + i:41 + i]).then_inc(sem("score_exp"), 1)
                elif kind == "ptrans":
                    act.wait_ge(sem("ptrans_ps"), i + 1)
                    nc.scalar.activation(PTb[:, i % 2, 0:128].rearrange("p (k j c) -> p k j c", k=4, j=4),
                                         ps[:, 4, :].rearrange("p (k j c) -> p k j c", k=4, j=4)[:, :, :, 0:8], ACT.Copy).then_inc(sem("PT_act"), 1)
                elif kind == "dt":
                    act.wait_ge(sem("dt_dve"), 1)
                    nc.scalar.activation(dts[:, 144:192], dts[:, 96:144], ACT.Exp, scale=-1.0).then_inc(sem("dt_act"), 1)
                    act.wait_ge(sem("dt_dve"), 2)
                    nc.scalar.activation(dts[:, 192:240], dts[:, 96:144], ACT.Ln).then_inc(sem("dt_act"), 1)
                elif kind == "conv_out":
                    act.wait_ge(sem("silu_ready"), CT)
                    act.wait_ge(sem("conv_out_ps"), 2 * i + 2)
                    nc.scalar.activation(conv_o_s[:, 512 * i:512 * i + 512], ps[0:DB * 7, 6 - 2 * (i % 2) + 1, :], ACT.Copy).then_inc(sem("conv_o_act"), 1)
                elif kind == "p_score":
                    act.wait_ge(sem("ps_biased"), i + 1)
                    nc.scalar.activation(Pp[:, i % 2, 0:P], Pp[:, i % 2, 0:P], ACT.Exp, bias=stat2(i, 0), accum_out=stat2(i, 2))
                    nc.scalar.activation(Pp[:, i % 2, P:3 * P], Pp[:, i % 2, P:3 * P], ACT.Exp, bias=stat2(i, 1), accum_out=stat2(i, 3)).then_inc(sem("pp_exp"), 1)
                elif kind == "p_trans":
                    act.wait_ge(sem("ppT_ps"), i + 1)
                    nc.scalar.activation(PTp[:, i % 2, :], ps[:, 6, 0:3 * P], ACT.Copy).then_inc(sem("ppT_act"), 1)

            batch = 0
            for c in range(3):
                n = ROWS[c]
                act.wait_ge(sem("cs_ready"), c + 1)
                nc.scalar.activation(ex[0:n], ex[0:n], ACT.Exp).then_inc(sem("ex_ready"), 1)
                for hb in range(4):
                    act.wait_ge(sem("seg_ps"), batch + 1)
                    if batch >= 2:
                        act.wait_ge(sem("M_ready"), batch - 1)
                    nc.scalar.activation(d3(Lb[batch % 2], P)[0:n, :, 0:n], d3(ps[:, 2 + batch % 2, :], P)[0:n, :, 0:n], ACT.Exp).then_inc(sem("L_ready"), 1)
                    batch += 1
                if c == 1:
                    act.wait_ge(sem("fin_ps"), 1)
                    nc.scalar.activation(fin_nat, ps[:, 6:8, :].rearrange("p a b -> p (a b)"), ACT.Copy).then_inc(sem("fin_ready"), 1)
                    act.wait_ge(sem("fin_ready"), 1)
                    act.dma_start(o["ssm_prompt"].rearrange("(j h) p n -> (h p) j n", j=8), d3(fin_nat, N)).then_inc(sem("fin_out"), 16)
            for b in range(DB):
                act.wait_ge(sem("stT_ps"), b + 1)
                nc.scalar.activation(stT, ps[:, 0:2, :].rearrange("p a b -> p (a b)"), ACT.Copy).then_inc(sem("stT_ready"), 1)
            act.wait_ge(sem("decay_ps"), 1)
            nc.scalar.activation(edx, ps[:, 2, 0:64], ACT.Exp).then_inc(sem("edx_ready"), 1)

            act.wait_ge(sem("mix_ss"), 1)
            nc.scalar.activation(dts[:, 0:9], stat[:, 0:9], ACT.Sqrt).then_inc(sem("mix_rt"), 1)
            act.wait_ge(sem("mix_rstd"), 1)
            for c in range(3):
                n = ROWS[c]
                for g in range(G):
                    nc.scalar.activation(y[0:n, c, 512 * g:512 * g + 512], y[0:n, c, 512 * g:512 * g + 512], ACT.Copy, scale=dts[0:n, 16 + 3 * c + g:17 + 3 * c + g])
                nc.scalar.activation(att[0:n, c, :], att[0:n, c, :], ACT.Copy, scale=dts[0:n, 18 + 3 * c:19 + 3 * c]).then_inc(sem("mix_ready"), 1)
            for k in range(1, 12, 2):
                act.wait_ge(sem("mixT_ps"), k + 1)
                nc.scalar.activation(mixT[:, k, :], ps[:, k % 2, 0:TOK], ACT.Copy, scale=vecs[:, 16 + k:17 + k]).then_inc(sem("mixT_act"), 1)

            norm_rows(1)
            xT_evac(1, 8)
            act.wait_ge(sem("top_ready"), 1)
            for i in range(3):
                n = ROWS[i]
                ins = nc.scalar.activation(e4[0:n, i, :], top8[0:n, i, 0:4], ACT.Exp, bias=rs1[0:n, i:i + 1])
            ins.then_inc(sem("e4_ready"), 1)

            act.wait_ge(sem("moe_free"), 1)
            act.wait_ge(sem("gateT_ps"), 1)
            nc.scalar.activation(GT[0:NE], ps[0:NE, 5, 0:TOK], ACT.Copy).then_inc(sem("GT_ready"), 1)

            act.wait_ge(sem("passes_ready"), 1)
            npass = act.value_load(passes_i, min_val=1, max_val=MAX_PASS)
            with act.Fori(0, npass) as p:
                with act.Fori(0, PAIRS) as pair:
                    pt = p * PAIRS + pair
                    for u in range(2):
                        act.wait_ge(sem("glu_ready"), 2 * pt + (u + 1))
                        nc.scalar.activation(sg, xg, ACT.Sigmoid, scale=ALPHA).then_inc(sem("sig_ready"), 1)
                        act.wait_ge(sem("gT_ps"), 2 * pt + (u + 1))
                        nc.scalar.activation(gT, ps[:, 5 * u, :], ACT.Copy).then_inc(sem("gT_ready"), 1)
                        if u == 0:
                            act.wait_ge(sem("GT_ps"), pt + 2)
                            nc.scalar.activation(GT, ps[:, 3, 0:TOK], ACT.Copy).then_inc(sem("GT_ready"), 1)
                        act.wait_ge(sem("expert_slot_used"), 2 * RING * pt + (2 + u) * RING)
                        for half in range(2):
                            nc.scalar.activation(ysb[C * u:C * u + C, 512 * half:512 * half + 512],
                                                 ps[C * half:C * half + C, 4, :], ACT.Copy).then_inc(sem("ysb_ready"), 1)

            act.wait_ge(sem("ss_ready"), 9)
            nc.scalar.activation(stat[:, 16:19], stat[:, 0:3], ACT.Sqrt).then_inc(sem("rt_ready"), 1)

        @block.vector
        def _(dve):
            chain = [0]

            def link(ins):
                chain[0] += 1
                ins.then_inc(sem("dve_link"), 1)
                dve.wait_ge(sem("dve_link"), chain[0])

            def both(bank):
                return ps[:, bank:bank + 2, :].rearrange("p a b -> p (a b)")

            def row_sums(call):
                for i in range(3):
                    n = ROWS[i]
                    nc.vector.tensor_tensor_reduce(xn[0:n, i, :], h[0:n, i, :], h[0:n, i, :], 1.0 / D, EPS,
                                                   ALU.mult, ALU.add, stat[0:n, i:i + 1]).then_inc(sem("ss_ready"), 1)

            def row_rstd(call):
                dve.wait_ge(sem("rt_ready"), call + 1)
                nc.vector.reciprocal(stat[:, 20:23], stat[:, 16:19]).then_inc(sem("rstd_ready"), 1)

            def xT_evac(call, g0):
                for k in range(0, KT, 2):
                    dve.wait_ge(sem("xnT_ps"), call * KT + k + 1)
                    nc.vector.tensor_scalar(xnT[:, k, :], ps[:, k % 2, 0:TOK], vecs[:, g0 + k:g0 + k + 1], None, ALU.mult).then_inc(sem("xnT_dve"), 1)

            dve.wait_ge(zeroed, 3)
            dve.wait_ge(sem("x_in"), 32)
            row_sums(0)
            dve.wait_ge(sem("vecs_ps"), 1)
            nc.vector.tensor_copy(vecs, ps[:, 7, 0:28]).then_inc(sem("vec_ready"), 1)
            nc.vector.tensor_copy(bvec, ps[:, 7, 32:112]).then_inc(sem("bvec_ready"), 1)
            row_rstd(0)
            xT_evac(0, 0)
            dve.wait_ge(sem("misc_ps"), 1)
            link(nc.vector.tensor_copy(cw, d3(ps[:, 6, 0:CT * 29], 29)))
            for i in range(CT):
                ins = nc.vector.tensor_copy(d3(xbcP[:, i, XS0:XP], 7)[:, :, 0:3], d3(cw[:, i, 0:24], 3))
            link(ins)
            dve.wait_ge(sem("ea_ready"), 1)
            link(nc.vector.tensor_scalar(bvec[:, 16:32], bvec[:, 16:32], -1.0, None, ALU.mult))
            dve.wait_ge(zeroed, 1)
            for kind, i in STEPS:
                if kind == "proj" and i % 2 == 1:
                    what, j, _ = TILES[i]
                    dve.wait_ge(sem("slot_used"), ITEM_AT[("w_in", i - 1)] + 1)
                    src = ps[:, i % 2, 0:TOK]
                    if what == "q":
                        nc.vector.tensor_scalar(qT[:, j, :], src, AE ** -0.5, None, ALU.mult).then_inc(sem("proj_out_dve"), 1)
                    elif what == "k":
                        nc.vector.tensor_copy(kT[:, j, :], src).then_inc(sem("proj_out_dve"), 1)
                    elif what == "x":
                        nc.vector.tensor_copy(xbcP[:, j, 3:XS0], src[:, 0:SEQ])
                        nc.vector.tensor_copy(d3(xbcP[:, j, XS0:XP], 7)[:, :, 3:7], d3(src[:, SEQ:TOK], DT)).then_inc(sem("proj_out_dve"), 1)
                    else:
                        u = UT.index(i)
                        if u >= 3:
                            dve.wait_ge(sem("nat_ps"), NAT.index(UT[u - 3]) + 1)
                        nc.vector.tensor_copy(utmp[:, u % 3, :], src).then_inc(sem("proj_out_dve"), 1)
                    if i == 3:
                        dve.wait_ge(zeroed, 4)
                        wait_proj_out(dve, 2)
                        wait_proj_out(dve, 3)
                        for j in range(4):
                            nc.vector.tensor_tensor(
                                Qz[:, :, j, 0:8].rearrange("p b (u t) -> p b u t", u=2),
                                d3(qT[:, j, SEQ:TOK], DT).unsqueeze(2).broadcast_to([P, DB, 2, DT]),
                                const("half").unsqueeze(1).unsqueeze(3).broadcast_to([P, DB, 2, DT]),
                                ALU.mult).then_inc(sem("Qz_ready"), 1)
                elif kind == "conv":
                    wait_proj_out(dve, 12 + i)
                    if i >= 2:
                        dve.wait_ge(sem("silu_ready"), i - 1)
                    t = conv_t[:, i % 2, :]
                    link(nc.vector.tensor_scalar(t, xbcP[:, i, 0:XC], cw[:, i, 24:25], cw[:, i, 28:29], ALU.mult, ALU.add))
                    for k in range(1, CONV):
                        ins = nc.vector.scalar_tensor_tensor(t, xbcP[:, i, k:k + XC], cw[:, i, 24 + k:25 + k], t, ALU.mult, ALU.add)
                        if k < CONV - 1:
                            link(ins)
                    ins.then_inc(sem("conv_ready"), 1)
                elif kind == "nat" and i in NAT_ON_DVE:
                    what, j, _ = TILES[NAT[i]]
                    dve.wait_ge(sem("nat_ps"), i + 1)
                    dst = {"k": k_nat, "v": v}[what]
                    nc.vector.tensor_copy(dst[:, 0:2, j * P:(j + 1) * P], d3(ps[:, 2, 0:2 * P], P))
                    nc.vector.tensor_copy(dst[0:NS, 2, j * P:(j + 1) * P], ps[0:NS, 2, 2 * P:3 * P]).then_inc(sem("nat_out_dve"), 1)
                elif kind == "ktrans":
                    if i == 0:
                        dve.wait_ge(sem("k_out"), 32)
                    for q in range(1, 8, 2):
                        half, j = q // 4, q % 4
                        if j < 3:
                            dve.wait_ge(sem("ktrans_ps"), 6 * i + 3 * half + j + 1)
                        else:
                            dve.wait_ge(sem("slot_used"), ITEM_AT[("k", i, half)] + 1)
                        nc.vector.tensor_copy(kTb[:, j, 512 * half:512 * half + 512], ps[:, 4 + q % 4, :]).then_inc(sem("ktrans_dve"), 1)
                elif kind == "score":
                    dve.wait_ge(sem("score_ps"), i + 1)
                    if i == 0:
                        dve.wait_ge(sem("bias_o_in"), 16)
                    nc.vector.tensor_tensor_reduce(Pb[:, i % 2, 0:PAST], both(6), bias_o, 1.0, NEG, ALU.add, ALU.max, stat[:, 24:25]).then_inc(sem("smax"), 1)
                    nc.vector.tensor_tensor_reduce(Pb[:, i % 2, PAST:PAST + NS], ps[:, 3, 0:NS], const("bias_new")[:, NS * i:NS * i + NS], 1.0, NEG,
                                                   ALU.add, ALU.max, stat[:, 25:26]).then_inc(sem("smax"), 1)
                    dve.wait_ge(sem("smax"), 2 * i + 2)
                    link(nc.vector.tensor_tensor(stat[:, 26:27], stat[:, 24:25], stat[:, 25:26], ALU.max))
                    nc.vector.tensor_scalar(stat[:, 32 + i:33 + i], stat[:, 26:27], -1.0, None, ALU.mult).then_inc(sem("score_biased"), 1)
                    dve.wait_ge(sem("score_exp"), i + 1)
                    link(nc.vector.reciprocal(stat[:, 48 + i:49 + i], stat[:, 40 + i:41 + i]))
                    nc.vector.tensor_scalar(Pb[:, i % 2, :], Pb[:, i % 2, :], stat[:, 48 + i:49 + i], None, ALU.mult).then_inc(sem("P_ready"), 1)
                elif kind == "ptrans":
                    dve.wait_ge(sem("ptrans_ps"), i + 1)
                    nc.vector.tensor_copy(PTb[:, i % 2, 128:256].rearrange("p (k j c) -> p k j c", k=4, j=4),
                                          ps[:, 5, :].rearrange("p (k j c) -> p k j c", k=4, j=4)[:, :, :, 0:8])
                    nc.vector.tensor_copy(d3(PTb[0:NS, i % 2, 256:288], 8), d3(ps[0:NS, 3, 128:256], 32)[:, :, 0:8]).then_inc(sem("PT_dve"), 1)
                elif kind == "pv":
                    dve.wait_ge(sem("pv_ps"), i + 1)
                    nc.vector.tensor_tensor(d3(OVm[:, i % 2, :], AE), d3(ps[:, 6, :], AE), const("head_of").unsqueeze(2).broadcast_to([P, AH, AE]),
                                            ALU.mult).then_inc(sem("OV_ready"), 1)
                elif kind == "gather_o":
                    dve.wait_ge(sem("go_ps"), i + 1)
                    if i == 0:
                        nc.vector.tensor_copy(att[0:NS, 2, :], ps[0:NS, 4, :]).then_inc(sem("att_s"), 1)
                    else:
                        dve.wait_ge(sem("att_s"), i)
                        nc.vector.tensor_tensor(att[0:NS, 2, :], ps[0:NS, 4, :], att[0:NS, 2, :], ALU.add).then_inc(sem("att_s"), 1)
                elif kind == "dt":
                    raw, dt, dA = dts[:, 240:288], dts[:, 0:48], dts[:, 48:96]
                    u1, e1, ln1 = dts[:, 96:144], dts[:, 144:192], dts[:, 192:240]
                    dve.wait_ge(zeroed, 2)
                    dve.wait_ge(sem("dt_ps"), 1)
                    link(nc.vector.tensor_tensor(d3(raw[:, 0:32], H), d3(ps[:, 3, 0:32], H), bvec[:, 0:16].unsqueeze(1).broadcast_to([P, 2, H]), ALU.add))
                    link(nc.vector.tensor_tensor(raw[0:NS, 32:48], ps[0:NS, 3, 32:48], bvec[0:NS, 0:16], ALU.add))
                    link(nc.vector.tensor_scalar(u1, raw, -1.0, None, ALU.mult))
                    nc.vector.tensor_tensor(u1, u1, raw, ALU.max).then_inc(sem("dt_dve"), 1)
                    dve.wait_ge(sem("dt_act"), 1)
                    nc.vector.tensor_scalar(u1, e1, 1.0, None, ALU.add).then_inc(sem("dt_dve"), 1)
                    dve.wait_ge(sem("dt_dve"), 2)
                    link(nc.vector.tensor_scalar(dt, u1, -1.0, None, ALU.add))
                    link(nc.vector.tensor_scalar(dA, dt, 0.0, None, ALU.is_equal))
                    link(nc.vector.tensor_tensor(dt, dt, dA, ALU.add))
                    link(nc.vector.tensor_tensor(dA, dA, e1, ALU.mult))
                    dve.wait_ge(sem("dt_act"), 2)
                    link(nc.vector.reciprocal(u1, dt))
                    link(nc.vector.tensor_tensor(u1, u1, e1, ALU.mult))
                    link(nc.vector.tensor_tensor(u1, u1, ln1, ALU.mult))
                    link(nc.vector.tensor_tensor(u1, u1, dA, ALU.add))
                    link(nc.vector.scalar_tensor_tensor(dt, raw, 0.0, u1, ALU.max, ALU.add))
                    nc.vector.tensor_tensor(d3(dA, H), d3(dt, H), bvec[:, 16:32].unsqueeze(1).broadcast_to([P, 3, H]), ALU.mult).then_inc(sem("dt_ready"), 1)
                elif kind == "conv_out":
                    dve.wait_ge(sem("silu_ready"), CT)
                    dve.wait_ge(sem("conv_out_ps"), 2 * i + 1)
                    nc.vector.tensor_copy(conv_o3[:, 512 * i:512 * i + 512], ps[0:3, 6 - 2 * (i % 2), :]).then_inc(sem("conv_o_dve"), 1)
                elif kind == "p_score":
                    if i == 0:
                        dve.wait_ge(sem("bias_p_in"), 16)
                    dve.wait_ge(sem("pps_ps"), i + 1)
                    if i >= 2:
                        dve.wait_ge(sem("ppT_ps"), i - 1)
                    if i:
                        dve.wait_ge(sem("ps_biased"), i)
                    bank = 4 + i % 2
                    nc.vector.tensor_tensor_reduce(Pp[:, i % 2, 0:P], ps[:, bank, 0:P], bias_p[:, i, P:2 * P], 1.0, NEG,
                                                   ALU.add, ALU.max, stat[:, 24:25]).then_inc(sem("pmax"), 1)
                    nc.vector.tensor_tensor_reduce(Pp[:, i % 2, P:3 * P], ps[:, bank, P:3 * P], bias_p[:, i, :], 1.0, NEG,
                                                   ALU.add, ALU.max, stat[:, 25:26]).then_inc(sem("pmax"), 1)
                    dve.wait_ge(sem("pmax"), 2 * i + 2)
                    link(nc.vector.tensor_scalar(stat2(i, 0), stat[:, 24:25], -1.0, None, ALU.mult))
                    nc.vector.tensor_scalar(stat2(i, 1), stat[:, 25:26], -1.0, None, ALU.mult).then_inc(sem("ps_biased"), 1)

            dve.wait_ge(sem("pav_ps"), 1)
            link(nc.vector.reciprocal(st4[:, 16:32], st4[:, 16:32]))
            for i in range(2):
                nc.vector.tensor_tensor(d3(att[:, i, :], AE), d3(ps[:, 3 + 4 * i, :], AE), st4[:, 16 + 8 * i:24 + 8 * i].unsqueeze(2).broadcast_to([P, AH, AE]),
                                        ALU.mult).then_inc(sem("att_prompt_out"), 1)
            dve.wait_ge(sem("att_prompt_out"), 2)
            for i in range(3):
                n = ROWS[i]
                link(nc.vector.tensor_tensor_reduce(tmp1[0:n, 0:AW], att[0:n, i, :], att[0:n, i, :], 1.0 / AW, EPS,
                                                    ALU.mult, ALU.add, stat[0:n, 3 * i + 2:3 * i + 3]))

            dve.wait_ge(sem("v_out"), 32)
            for c in range(3):
                n = ROWS[c]
                dve.wait_ge(sem("gram_ps"), c + 1)
                link(nc.vector.tensor_tensor(d3(GM, P)[0:n, :, 0:n], d3(ps[:, 0, 0:2 * P], P)[0:n, :, 0:n],
                                             le(c).unsqueeze(1).broadcast_to([n, G, n]), ALU.mult))
                if c >= 1:
                    dve.wait_ge(sem("Xd_ready"), c)
                link(nc.vector.tensor_copy(ex[0:n, 16:48], ps[0:n, 1, 0:32]))
                nc.vector.tensor_tensor(ex[0:n, 0:16], ex[0:n, 32:48], ex[0:n, 16:32], ALU.subtract).then_inc(sem("cs_ready"), 1)
                for hb in range(4):
                    batch = 4 * c + hb
                    dve.wait_ge(sem("L_ready"), batch + 1)
                    if batch >= 2:
                        dve.wait_ge(sem("yd_ps"), batch - 1)
                    nc.vector.tensor_tensor(d3(Mb[batch % 2], P)[0:n, :, 0:n], d3(Lb[batch % 2], P)[0:n, :, 0:n],
                                            GM[0:n, (hb // 2) * P:(hb // 2) * P + n].unsqueeze(1).broadcast_to([n, 4, n]),
                                            ALU.mult).then_inc(sem("M_ready"), 1)
                yc = y[0:n, c, :]
                dve.wait_ge(sem("yd_ps"), 4 * c + 4)
                dve.wait_ge(sem("DX_ready"), c + 1)
                nc.vector.tensor_tensor(yc, yc, both(4)[0:n], ALU.add).then_inc(sem("yd_out"), 1)
                dve.wait_ge(sem("yd_out"), c + 1)
                if c >= 1:
                    dve.wait_ge(sem("yo_ps"), c)
                    dve.wait_ge(sem("ex_ready"), c + 1)
                    nc.vector.tensor_tensor(d3(tmp1[0:n], HP), d3(both(6)[0:n], HP), ex[0:n, 16:32].unsqueeze(2).broadcast_to([n, H, HP]),
                                            ALU.mult).then_inc(sem("yo_out"), 1)
                    dve.wait_ge(sem("yo_out"), c)
                    link(nc.vector.tensor_tensor(yc, yc, tmp1[0:n], ALU.add))
                if c == 0:
                    dve.wait_ge(sem("st_ps"), 1)
                    nc.vector.tensor_copy(St, both(6)).then_inc(sem("St_ready"), 1)
                if c == 1:
                    dve.wait_ge(sem("st_ps"), 2)
                    link(nc.vector.tensor_tensor(d3(St, HP), d3(St, HP), ex[:, 32:48].unsqueeze(2).broadcast_to([P, H, HP]), ALU.mult))
                    nc.vector.tensor_tensor(St, St, both(6), ALU.add).then_inc(sem("St_ready"), 1)
                if c == 0:
                    wait_nat_out(dve, len(NAT) - 1)
                link(nc.vector.tensor_tensor(yc, yc, z[0:n, c, :], ALU.mult))
                for g in range(G):
                    link(nc.vector.tensor_tensor_reduce(tmp1[0:n, 0:512], yc[:, 512 * g:512 * g + 512], yc[:, 512 * g:512 * g + 512], 1.0 / 512, EPS,
                                                        ALU.mult, ALU.add, stat[0:n, 3 * c + g:3 * c + g + 1]))
            dve.wait_ge(sem("edx_ready"), 1)
            for j in range(8):
                dve.wait_ge(sem("fs_ps"), j + 1)
                dve.wait_ge(sem("state_new"), j)
                link(nc.vector.tensor_tensor(d3(tmp1, N), state[:, :, j, :], edx[:, 8 * j:8 * j + 8].unsqueeze(2).broadcast_to([P, DB, N]), ALU.mult))
                nc.vector.tensor_tensor(state[:, :, j, :], d3(tmp1, N), d3(both(4 + 2 * (j % 2)), N), ALU.add).then_inc(sem("state_new"), 1)
            dve.wait_ge(sem("state_new"), 8)
            nc.vector.tensor_copy(stat[:, 27:28], stat[:, 0:1]).then_inc(sem("work_free"), 1)
            nc.vector.tensor_copy(stat[:, 28:29], stat[:, 0:1]).then_inc(sem("mix_ss"), 1)
            dve.wait_ge(sem("mix_rt"), 1)
            nc.vector.reciprocal(dts[:, 16:25], dts[:, 0:9]).then_inc(sem("mix_rstd"), 1)
            for k in range(0, 12, 2):
                dve.wait_ge(sem("mixT_ps"), k + 1)
                nc.vector.tensor_scalar(mixT[:, k, :], ps[:, k % 2, 0:TOK], vecs[:, 16 + k:17 + k], None, ALU.mult).then_inc(sem("mixT_dve"), 1)

            dve.wait_ge(sem("expert_slot_used"), RING)
            nc.vector.tensor_tensor(h[:, 0, :], h[:, 0, :], both(2), ALU.add)
            nc.vector.tensor_tensor(h[:, 1, :], h[:, 1, :], both(4), ALU.add)
            nc.vector.tensor_tensor(h[0:NS, 2, 0:512], h[0:NS, 2, 0:512], ps[0:NS, 6, :], ALU.add)
            link(nc.vector.tensor_tensor(h[0:NS, 2, 512:D], h[0:NS, 2, 512:D], ps[NS:2 * NS, 6, :], ALU.add))
            row_sums(1)
            row_rstd(1)
            xT_evac(1, 8)

            dve.wait_ge(zeroed, 5)
            dve.wait_ge(sem("logit_ps"), 1)
            nc.vector.tensor_tensor(logit[:, 0:2, :], d3(ps[:, 2, 0:2 * NE], NE), bvec[:, 48:80].unsqueeze(1).broadcast_to([P, 2, NE]), ALU.add)
            link(nc.vector.tensor_tensor(logit[0:NS, 2, :], ps[0:NS, 2, 2 * NE:3 * NE], bvec[0:NS, 48:80], ALU.add))
            for i in range(3):
                ins = nc.vector.max(top8[0:ROWS[i], i, :], logit[0:ROWS[i], i, :])
            link(ins)
            for i in range(3):
                n = ROWS[i]
                nc.vector.max_index(idx8[0:n, i, :].bitcast(U32), top8[0:n, i, :], logit[0:n, i, :])
                ins = nc.vector.tensor_scalar(rs1[0:n, i:i + 1], top8[0:n, i, 0:1], -1.0, None, ALU.mult)
            ins.then_inc(sem("top_ready"), 1)
            dve.wait_ge(sem("top_ready"), 1)
            for i in range(3):
                ins = nc.vector.tensor_copy(idxf[0:ROWS[i], i, :], idx8[0:ROWS[i], i, :].bitcast(U32))
            link(ins)
            dve.wait_ge(sem("e4_ready"), 1)
            for i in range(3):
                n = ROWS[i]
                ins = nc.vector.tensor_reduce(rs1[0:n, i:i + 1], e4[0:n, i, :], AX_X, ALU.add)
            link(ins)
            for i in range(3):
                ins = nc.vector.reciprocal(rs1[0:ROWS[i], i:i + 1], rs1[0:ROWS[i], i:i + 1])
            link(ins)
            for i in range(3):
                n = ROWS[i]
                ins = nc.vector.tensor_scalar(e4[0:n, i, :], e4[0:n, i, :], rs1[0:n, i:i + 1], None, ALU.mult)
            link(ins)
            for i in range(3):
                n = ROWS[i]
                expert = const("expert", n)
                for j in range(TOPK):
                    pick, weight = idxf[0:n, i, j:j + 1], e4[0:n, i, j:j + 1]
                    if j == 0:
                        nc.vector.tensor_scalar(mask[0:n, i, :], expert, pick, None, ALU.is_equal)
                        link(nc.vector.tensor_scalar(gate[0:n, i, 0:NE], expert, pick, weight, ALU.is_equal, ALU.mult))
                    else:
                        link(nc.vector.tensor_scalar(eq1[0:n], expert, pick, None, ALU.is_equal))
                        nc.vector.tensor_tensor(mask[0:n, i, :], mask[0:n, i, :], eq1[0:n], ALU.add)
                        link(nc.vector.scalar_tensor_tensor(gate[0:n, i, 0:NE], eq1[0:n], weight, gate[0:n, i, 0:NE], ALU.mult, ALU.add))
            nc.vector.tensor_copy(stat[:, 27:28], stat[:, 0:1]).then_inc(sem("mask_ready"), 1)
            dve.wait_ge(sem("pos_ps"), 1)
            nc.vector.scalar_tensor_tensor(posm[:, 0:2, 0:NE], d3(ps[:, 3, 0:2 * NE], NE), 1.0, mask[:, 0:2, :], ALU.add, ALU.mult)
            link(nc.vector.scalar_tensor_tensor(posm[0:NS, 2, 0:NE], ps[0:NS, 3, 2 * NE:3 * NE], 1.0, mask[0:NS, 2, :], ALU.add, ALU.mult))
            nc.vector.tensor_scalar(posm[:, 0:2, :], posm[:, 0:2, :], -1.0, None, ALU.add).then_inc(sem("pos_shifted"), 1)
            nc.vector.tensor_scalar(posm[0:NS, 2, :], posm[0:NS, 2, :], -1.0, None, ALU.add).then_inc(sem("pos_shifted"), 1)
            link(nc.vector.tensor_reduce(passes[0:1, 0:1], ps[0:1, 3, 3 * NE:4 * NE], AX_X, ALU.max))
            nc.vector.tensor_copy(stat[:, 28:29], stat[:, 0:1]).then_inc(sem("hid_read"), 1)
            nc.vector.tensor_copy(stat[:, 29:30], stat[:, 0:1]).then_inc(sem("comb_read"), 4)
            nc.vector.tensor_copy(stat[:, 30:31], stat[:, 0:1]).then_inc(sem("xT_ready"), 1)
            for k in range(1, MAX_PASS):
                ins = nc.vector.tensor_scalar(passes[0:1, k:k + 1], passes[0:1, 0:1], float(C * k), None, ALU.is_gt)
            link(ins)
            link(nc.vector.tensor_reduce(passes[0:1, 6:7], passes[0:1, 1:MAX_PASS], AX_X, ALU.add))
            link(nc.vector.tensor_scalar(passes[0:1, 7:8], passes[0:1, 6:7], 1.0, None, ALU.add))
            nc.vector.tensor_copy(passes_i, passes[0:1, 7:8]).then_inc(sem("passes_ready"), 1)
            dve.wait_ge(sem("passes_ready"), 1)

            def add_outputs():
                nc.vector.tensor_tensor(h[0:NS, 2, 0:512], h[0:NS, 2, 0:512], ps[0:NS, 5, :], ALU.add).then_inc(sem("comb_read"), 1)
                nc.vector.tensor_tensor(h[0:NS, 2, 512:D], h[0:NS, 2, 512:D], ps[NS:2 * NS, 5, :], ALU.add).then_inc(sem("comb_read"), 1)
                nc.vector.tensor_tensor(h[:, 1, :], h[:, 1, :], both(3), ALU.add).then_inc(sem("comb_read"), 1)
                nc.vector.tensor_tensor(h[:, 0, :], h[:, 0, :], both(6), ALU.add).then_inc(sem("comb_read"), 1)

            def pair_views(e, rows, tiles):
                n = tiles.stop - tiles.start
                shape = [rows, n, 2, C]
                places, weights = (t[0:rows, tiles, bass.ds(e, 2)].unsqueeze(3).broadcast_to(shape) for t in (posm, gate))
                s1, s2 = (t[0:rows, tiles].rearrange("p i (u c) -> p i u c", u=2) for t in (S1, S2))
                slots = const("slot", rows)[:, 0:C].unsqueeze(1).unsqueeze(1).broadcast_to(shape)
                return places, weights, slots, s1, s2

            def build_selections(e, builds):
                for rows, tiles in ((P, slice(0, 2)), (NS, slice(2, 3))):
                    places, _, slots, s1, _ = pair_views(e, rows, tiles)
                    nc.vector.tensor_tensor(s1, slots, places, ALU.is_equal).then_inc(sem("S_ready"), 1)
                dve.wait_ge(sem("S_ready"), 4 * builds + 2)
                for rows, tiles in ((P, slice(0, 2)), (NS, slice(2, 3))):
                    _, weights, _, s1, s2 = pair_views(e, rows, tiles)
                    nc.vector.tensor_tensor(s2, s1, weights, ALU.mult).then_inc(sem("S_ready"), 1)

            def build_b1_rows(e):
                nc.vector.tensor_copy(sel[0:96], const("expert_row", 96)[:, bass.ds(e, 2)].unsqueeze(2).broadcast_to([96, 2, C])).then_inc(sem("sel_ready"), 1)

            def expert_inputs(gathers, u):
                dve.wait_ge(sem("gather_ps"), gathers)
                nc.vector.tensor_tensor(d3(xT, C), d3(ps[:, 5 * u, :], C), vecs[:, 8:16].unsqueeze(2).broadcast_to([P, KT, C]), ALU.mult).then_inc(sem("xT_ready"), 1)

            dve.wait_ge(sem("moe_free"), 1)
            npass = dve.value_load(passes_i, min_val=1, max_val=MAX_PASS)
            with dve.Fori(0, npass) as p:
                dve.wait_ge(sem("pos_shifted"), 2 * p + 2)
                dve.wait_ge(sem("gather_ps"), p * (NE + 1) + 1)
                dve.wait_ge(sem("GT_ps"), p * PAIRS + 1)
                dve.wait_ge(sem("hid_read"), p * NE + 1)
                build_selections(0, p * (PAIRS + 1))
                build_b1_rows(0)
                expert_inputs(p * (NE + 1) + 2, 0)
                with dve.Fori(0, PAIRS) as pair:
                    pt = p * PAIRS + pair
                    for u in range(2):
                        et = 2 * pt + u
                        dve.wait_ge(sem("expert_slot_used"), 2 * RING * pt + (RING * u + RING + KT))
                        hid = d3(both(1), 2)
                        nc.vector.tensor_scalar(xg, hid[:, :, 0], LIMIT, None, ALU.min).then_inc(sem("glu_ready"), 1)
                        nc.vector.tensor_scalar(xl, hid[:, :, 1], -LIMIT, LIMIT, ALU.max, ALU.min).then_inc(sem("hid_read"), 1)
                        dve.wait_ge(sem("hid_read"), et + 2)
                        nc.vector.scalar_tensor_tensor(xl, xl, 1.0, xg, ALU.add, ALU.mult).then_inc(sem("lin_glu"), 1)
                        dve.wait_ge(sem("lin_glu"), et + 1)
                        dve.wait_ge(sem("sig_ready"), et + 1)
                        nc.vector.tensor_tensor(gg, xl, sg, ALU.mult).then_inc(sem("g_ready"), 1)
                        if u == 0:
                            dve.wait_ge(sem("comb_ps"), pt + 1)
                            dve.wait_ge(sem("comb_read"), 4 * pt + 4)
                            add_outputs()
                        expert_inputs(p * (NE + 1) + 2 * pair + (3 + u), 1 - u)
                        if u == 0:
                            dve.wait_ge(sem("GT_ps"), pt + 2)
                            build_selections(2 * pair + 2, p * (PAIRS + 1) + pair + 1)
                        else:
                            build_b1_rows(2 * pair + 2)
                nc.vector.tensor_scalar(posm[:, 0:2, :], posm[:, 0:2, :], float(-C), None, ALU.add).then_inc(sem("pos_shifted"), 1)
                nc.vector.tensor_scalar(posm[0:NS, 2, :], posm[0:NS, 2, :], float(-C), None, ALU.add).then_inc(sem("pos_shifted"), 1)
            dve.wait_ge(sem("comb_ps"), npass * PAIRS + 1)
            dve.wait_ge(sem("comb_read"), npass * (4 * PAIRS) + 4)
            add_outputs()
            dve.wait_ge(sem("comb_read"), npass * (4 * PAIRS) + 8)

            row_sums(2)
            row_rstd(2)
            dve.wait_ge(sem("rstd_ready"), 3)
            dve.wait_ge(sem("nfin_in"), 16)
            for i in range(3):
                n = ROWS[i]
                nc.vector.scalar_tensor_tensor(h[0:n, i, :], h[0:n, i, :], stat[0:n, 20 + i:21 + i], nfin[0:n], ALU.mult, ALU.mult).then_inc(sem("y_final"), 1)

        @block.tensor
        def _(pe):
            pe.wait_ge(sem("const_in"), 16)
            pe.wait_ge(sem("vec_in"), 16 * 8)
            nc.tensor.transpose(ps[:, 7, 0:28], rows_small[0:28, 0:P], ident[0:28, 0:28])
            nc.tensor.matmul(ps[:, 7, 32:112], const("ones")[0:1, :], rows_small[0:1, P:P + 80], start=True, stop=True).then_inc(sem("vecs_ps"), 1)

            def transposed_tokens(call):
                pe.wait_ge(sem("xn_ready"), 3 * call + 3)
                for k in range(KT):
                    if k >= 2:
                        pe.wait_ge(sem("xnT_dve" if k % 2 == 0 else "xnT_act"), 4 * call + k // 2)
                    for c in range(3):
                        last = nc.tensor.transpose(ps[:, k % 2, cols(c)], xn[0:ROWS[c], c, k * P:(k + 1) * P], ident[0:ROWS[c], 0:ROWS[c]])
                    last.then_inc(sem("xnT_ps"), 1)
                pe.wait_ge(sem("xnT_dve"), 4 * call + 4)
                pe.wait_ge(sem("xnT_act"), 4 * call + 4)

            transposed_tokens(0)
            pe.wait_ge(sem("rows_in"), 48)
            for i in range(CT):
                last = nc.tensor.transpose(ps[:, 6, 29 * i:29 * i + 29], rows29[0:29, P * i:P * i + P], ident[0:29, 0:29])
            last.then_inc(sem("misc_ps"), 1)
            for kind, i in STEPS:
                if kind == "proj":
                    item = ("w_in", i - i % 2)
                    if i % 2 == 0:
                        mix_full(pe, item)
                    if i >= 2:
                        wait_proj_out(pe, i - 2)
                    w = d3(slot(ITEM_AT[item] % MIX_RING), 2 * P)
                    for k in range(KT):
                        last = nc.tensor.matmul(ps[:, i % 2, 0:TOK], w[:, k, (i % 2) * P:(i % 2) * P + P], xnT[:, k, :], start=(k == 0), stop=(k == KT - 1))
                    last.then_inc(sem("slot_used" if i % 2 else "proj_ps"), 1)
                elif kind == "nat":
                    n = NAT[i]
                    what, j, _ = TILES[n]
                    if what == "x":
                        pe.wait_ge(sem("silu_ready"), j + 1)
                        src = xbcT[:, j, :]
                    else:
                        wait_proj_out(pe, n)
                        src = kT[:, j, :] if what == "k" else utmp[:, UT.index(n) % 3, :]
                    if i:
                        wait_nat_out(pe, i - 1)
                    for c in range(3):
                        last = nc.tensor.transpose(ps[0:ROWS[c], 2, c * P:(c + 1) * P], src[:, cols(c)], ident)
                    last.then_inc(sem("nat_ps"), 1)
                elif kind == "ktrans":
                    if i >= 2:
                        pe.wait_ge(sem("att_s"), i - 1)
                    for half in range(2):
                        mix_full(pe, ("k", i, half))
                        kc = d3(slot(ITEM_AT[("k", i, half)] % MIX_RING), AW)
                        for j in range(4):
                            q = 4 * half + j
                            if q == 2 and i:
                                pe.wait_ge(sem("score_biased"), i)
                            if q >= 4:
                                pe.wait_ge(sem("ktrans_act" if q % 2 == 0 else "ktrans_dve"), 4 * i + q // 2 - 1)
                            for m in range(4):
                                last = nc.tensor.transpose(ps[:, 4 + q % 4, m * P:(m + 1) * P], kc[:, m, j * P:(j + 1) * P], ident)
                            last.then_inc(sem("ktrans_ps" if j < 3 else "slot_used"), 1)
                elif kind == "score":
                    pe.wait_ge(sem("Qz_ready"), 4)
                    pe.wait_ge(sem("ktrans_act"), 4 * i + 4)
                    pe.wait_ge(sem("ktrans_dve"), 4 * i + 4)
                    if i:
                        pe.wait_ge(sem("OV_ready"), i)
                    else:
                        for n in range(4, 8):
                            wait_proj_out(pe, n)
                    for half in range(2):
                        for j in range(4):
                            nc.tensor.matmul(ps[32 * j:32 * j + 32, 6 + half, :], Qz[:, i, j, :], kTb[:, j, 512 * half:512 * half + 512], start=True, stop=True)
                    for j in range(4):
                        last = nc.tensor.matmul(ps[32 * j:32 * j + 32, 3, 0:NS], Qz[:, i, j, :], kT[:, j, SEQ:TOK], start=True, stop=True)
                    last.then_inc(sem("score_ps"), 1)
                elif kind == "ptrans":
                    pe.wait_ge(sem("P_ready"), i + 1)
                    if i + 1 < DB:
                        pe.wait_ge(sem("ktrans_act"), 4 * i + 8)
                        pe.wait_ge(sem("ktrans_dve"), 4 * i + 8)
                    else:
                        pe.wait_ge(sem("att_s"), i)
                    for k in range(8):
                        nc.tensor.transpose(ps[:, 4 + k // 4, (k % 4) * P:(k % 4 + 1) * P], Pb[:, i % 2, k * P:(k + 1) * P], ident)
                    nc.tensor.transpose(ps[0:NS, 3, 128:256], Pb[:, i % 2, PAST:PAST + NS], ident).then_inc(sem("ptrans_ps"), 1)
                elif kind == "pv":
                    pe.wait_ge(sem("PT_act"), i + 1)
                    pe.wait_ge(sem("PT_dve"), i + 1)
                    if i == 0:
                        for n in range(4, 8):
                            wait_nat_out(pe, n)
                    for half in range(2):
                        mix_full(pe, ("v", i, half))
                        vc = d3(slot(ITEM_AT[("v", i, half)] % MIX_RING), AW)
                        for m in range(4):
                            k = 4 * half + m
                            last = nc.tensor.matmul(ps[32 * m:32 * m + 32, 6, :], PTb[:, i % 2, k * 32:k * 32 + 32], vc[:, m, :],
                                                    start=(half == 0), stop=(half == 1 and m > 0))
                        last.then_inc(sem("slot_used"), 1)
                    nc.tensor.matmul(ps[0:32, 6, :], PTb[0:NS, i % 2, 256:288], v[0:NS, 2, :], start=False, stop=True).then_inc(sem("pv_ps"), 1)
                elif kind == "gather_o":
                    pe.wait_ge(sem("OV_ready"), i + 1)
                    nc.tensor.matmul(ps[0:NS, 4, :], const("to_token")[:, NS * i:NS * i + NS], OVm[:, i % 2, :], start=True, stop=True).then_inc(sem("go_ps"), 1)
                elif kind == "dt":
                    pe.wait_ge(sem("wdt_in"), 16)
                    for c in range(3):
                        for k in range(KT):
                            last = nc.tensor.matmul(ps[0:ROWS[c], 3, H * c:H * c + H], xnT[:, k, cols(c)], w_dt[:, k, :], start=(k == 0), stop=(k == KT - 1))
                    last.then_inc(sem("dt_ps"), 1)
                elif kind == "conv_out":
                    if i == 1:
                        pe.wait_ge(sem("att_s"), DB)
                    if i == 2:
                        pe.wait_ge(sem("conv_o_dve"), 1)
                        pe.wait_ge(sem("conv_o_act"), 1)
                    bank = 6 - 2 * (i % 2)
                    for m in range(4):
                        last = nc.tensor.transpose(ps[0:3, bank, m * P:(m + 1) * P], xbcP[:, 4 * i + m, XS0 - 3:XS0], ident)
                    last.then_inc(sem("conv_out_ps"), 1)
                    for m in range(4):
                        last = nc.tensor.transpose(ps[0:DB * 7, bank + 1, m * P:(m + 1) * P], xbcP[:, 4 * i + m, XS0:XP], ident)
                    last.then_inc(sem("conv_out_ps"), 1)
                elif kind == "p_score":
                    if i == 0:
                        pe.wait_ge(sem("conv_o_dve"), 2)
                        pe.wait_ge(sem("conv_o_act"), 2)
                    if i >= 2:
                        pe.wait_ge(sem("ps_biased"), i - 1)
                    r, j = slice(64 * (i % 2), 64 * (i % 2) + 64), i // 2
                    nc.tensor.matmul(ps[:, 4 + i % 2, 0:P], qT[r, j, 0:P], kT[r, j, 0:P], start=True, stop=True)
                    nc.tensor.matmul(ps[:, 4 + i % 2, P:3 * P], qT[r, j, P:2 * P], kT[r, j, 0:2 * P], start=True, stop=True).then_inc(sem("pps_ps"), 1)
                elif kind == "p_trans":
                    pe.wait_ge(sem("pp_exp"), i + 1)
                    if i == 0:
                        pe.wait_ge(sem("conv_o_dve"), 3)
                        pe.wait_ge(sem("conv_o_act"), 3)
                        pe.wait_ge(sem("dt_dve"), 1)
                    for m in range(3):
                        last = nc.tensor.transpose(ps[:, 6, m * P:(m + 1) * P], Pp[:, i % 2, m * P:(m + 1) * P], ident)
                    last.then_inc(sem("ppT_ps"), 1)
                elif kind == "p_out":
                    pe.wait_ge(sem("ppT_act"), i + 1)
                    c = slice(i * AE, i * AE + AE)
                    nc.tensor.matmul(ps[:, 3, c], PTp[:, i % 2, 0:P], v[:, 0, c], start=True, stop=True)
                    nc.tensor.matmul(ps[:, 7, c], PTp[:, i % 2, P:2 * P], v[:, 0, c], start=True, stop=False)
                    last = nc.tensor.matmul(ps[:, 7, c], PTp[:, i % 2, 2 * P:3 * P], v[:, 1, c], start=False, stop=True)
                    if i == AH - 1:
                        last.then_inc(sem("pav_ps"), 1)

            dA = dts[:, 48:96]
            pe.wait_ge(sem("att_prompt_out"), 2)
            pe.wait_ge(sem("dt_ready"), 1)
            for i in range(len(NAT)):
                wait_nat_out(pe, i)
            for c in range(3):
                n = ROWS[c]
                if c:
                    pe.wait_ge(sem("cs_ready"), c)
                for g in range(G):
                    nc.tensor.matmul(ps[0:n, 0, g * P:g * P + n], xbcT[:, 8 + g, cols(c)], xbcT[:, 10 + g, cols(c)], start=True, stop=True)
                nc.tensor.matmul(ps[0:n, 1, 0:H], le(c), dA[0:n, H * c:H * c + H], start=True, stop=True)
                nc.tensor.matmul(ps[0:n, 1, H:2 * H], same(c), dA[0:n, H * c:H * c + H], start=True, stop=True).then_inc(sem("gram_ps"), 1)

                def diagonal(batch):
                    pe.wait_ge(sem("M_ready"), batch + 1)
                    pe.wait_ge(sem("X_ready"), c + 1)
                    if batch % 4 == 0 and c:
                        pe.wait_ge(sem("yd_out"), c)
                    for u in range(4):
                        hd = 4 * (batch % 4) + u
                        last = nc.tensor.matmul(ps[0:n, 4 + hd // 8, (hd % 8) * HP:(hd % 8 + 1) * HP], d3(Mb[batch % 2], P)[0:n, u, 0:n],
                                                d3(Xh, HP)[0:n, hd, :], start=True, stop=True)
                    last.then_inc(sem("yd_ps"), 1)

                for hb in range(4):
                    batch = 4 * c + hb
                    pe.wait_ge(sem("dAm_ready"), batch + 1)
                    if batch >= 2:
                        pe.wait_ge(sem("L_ready"), batch - 1)
                    for u in range(4):
                        last = nc.tensor.matmul(ps[0:n, 2 + batch % 2, u * P:u * P + n], d3(dAm[batch % 2], P)[0:n, u, 0:n], le(c), start=True, stop=True)
                    last.then_inc(sem("seg_ps"), 1)
                    if hb:
                        diagonal(batch - 1)
                diagonal(4 * c + 3)

                def chunk_state():
                    pe.wait_ge(sem("Xd_ready"), c + 1)
                    for g in range(G):
                        last = nc.tensor.matmul(ps[:, 6 + g, :], Bn[:, c, g * N:(g + 1) * N], Xd[:, 512 * g:512 * g + 512], start=True, stop=True)
                    last.then_inc(sem("st_ps"), 1)

                if c == 0:
                    chunk_state()
                if c == 1:
                    pe.wait_ge(sem("St_ready"), 1)
                    for g in range(G):
                        last = nc.tensor.matmul(ps[:, 6 + g, :], xbcT[:, 10 + g, cols(c)], St[:, 512 * g:512 * g + 512], start=True, stop=True)
                    last.then_inc(sem("yo_ps"), 1)
                    pe.wait_ge(sem("yo_out"), 1)
                    chunk_state()
                    pe.wait_ge(sem("St_ready"), 2)
                    for j in range(8):
                        last = nc.tensor.transpose(ps[:, 6 + j // 4, (j % 4) * P:(j % 4 + 1) * P], St[:, j * P:(j + 1) * P], ident)
                    last.then_inc(sem("fin_ps"), 1)
            pe.wait_ge(sem("cs_ready"), 3)
            pe.wait_ge(sem("fin_ready"), 1)
            pe.wait_ge(sem("CTm_ready"), 2)
            for b in range(DB):
                pe.wait_ge(sem(f"state_in{b}"), 16)
                for j in range(8):
                    last = nc.tensor.transpose(ps[:, j // 4, (j % 4) * P:(j % 4 + 1) * P], state[:, b, j, :], ident)
                last.then_inc(sem("stT_ps"), 1)
                pe.wait_ge(sem("stT_ready"), b + 1)
                for g in range(G):
                    last = nc.tensor.matmul(ps[0:NS, 6 + g, :], CTm[g][:, NS * b:NS * b + NS], stT[:, 512 * g:512 * g + 512], start=(b == 0), stop=(b == DB - 1))
            last.then_inc(sem("yo_ps"), 1)
            pe.wait_ge(sem("dAx_ready"), 1)
            pe.wait_ge(sem("L_ready"), 12)
            for j in range(8):
                last = nc.tensor.matmul(ps[:, 2, 8 * j:8 * j + 8], dAx[0:NS, j * P:(j + 1) * P], const("seq_of", NS), start=True, stop=True)
                if j == 0:
                    last.then_inc(sem("expert_slot_used"), RING - MIX_RING)
            last.then_inc(sem("decay_ps"), 1)
            pe.wait_ge(sem("Bm_ready"), 2)
            pe.wait_ge(sem("Xd_ready"), 3)
            pe.wait_ge(sem("yd_out"), 3)
            pe.wait_ge(sem("yo_out"), 2)
            for j in range(8):
                if j >= 2:
                    pe.wait_ge(sem("state_new"), j - 1)
                for half in range(2):
                    last = nc.tensor.matmul(ps[:, 4 + 2 * (j % 2) + half, :], Xd[0:NS, j * P:(j + 1) * P],
                                            Bm[0:NS, j // 4, 4 * half:4 * half + 4, :].rearrange("p b n -> p (b n)"), start=True, stop=True)
                last.then_inc(sem("fs_ps"), 1)

            pe.wait_ge(sem("mix_ready"), 3)
            for k in range(12):
                if k >= 2:
                    pe.wait_ge(sem("mixT_dve" if k % 2 == 0 else "mixT_act"), k // 2)
                for c in range(3):
                    n = ROWS[c]
                    src = y[0:n, c, k * P:(k + 1) * P] if k < 8 else att[0:n, c, (k - 8) * P:(k - 7) * P]
                    last = nc.tensor.transpose(ps[:, k % 2, cols(c)], src, ident[0:n, 0:n])
                last.then_inc(sem("mixT_ps"), 1)
            pe.wait_ge(sem("mixT_dve"), 6)
            pe.wait_ge(sem("mixT_act"), 6)
            pe.wait_ge(sem("state_new"), 8)
            pe.wait_ge(sem("edx_ready"), 1)
            for k in range(12):
                i = k // 2
                if k % 2 == 0:
                    mix_full(pe, ("w_out", i))
                w = d3(slot(ITEM_AT[("w_out", i)] % MIX_RING), D)[:, k % 2, :]
                first, final = k == 0, k == 11
                for half in range(2):
                    for c in range(2):
                        nc.tensor.matmul(ps[:, 2 + 2 * c + half, :], mixT[:, k, cols(c)], w[:, 512 * half:512 * half + 512], start=first, stop=final)
                for half in range(2):
                    last = nc.tensor.matmul(ps[NS * half:NS * half + NS, 6, :], mixT[:, k, cols(2)], w[:, 512 * half:512 * half + 512], start=first, stop=final)
                if k == 1:
                    last.then_inc(sem("slot_used"), 1)
                if k % 2 == 1 and i >= 2:
                    last.then_inc(sem("expert_slot_used"), 2 if i == 5 else 1)

            transposed_tokens(1)
            pe.wait_ge(sem("wr_in"), 16)
            for c in range(3):
                for k in range(KT):
                    last = nc.tensor.matmul(ps[0:ROWS[c], 2, NE * c:NE * c + NE], xnT[:, k, cols(c)], w_router[:, k, :], start=(k == 0), stop=(k == KT - 1))
            last.then_inc(sem("logit_ps"), 1)
            pe.wait_ge(sem("mask_ready"), 1)
            for c in range(3):
                n = ROWS[c]
                for d in range(c):
                    nc.tensor.matmul(ps[0:n, 3, NE * c:NE * c + NE], const("ones")[:, 0:n], mask[:, d, :], start=(d == 0), stop=False)
                nc.tensor.matmul(ps[0:n, 3, NE * c:NE * c + NE], const("lt", n)[:, 0:n], mask[0:n, c, :], start=(c == 0), stop=True)
            for c in range(3):
                n = ROWS[c]
                last = nc.tensor.matmul(ps[0:1, 3, 3 * NE:4 * NE], const("ones", n)[:, 0:1], mask[0:n, c, :], start=(c == 0), stop=(c == 2))
                if c < 2:
                    last.then_inc(sem(("gather_ps", "GT_ps")[c]), 1)
            last.then_inc(sem("pos_ps"), 1)

            for c in range(3):
                n = ROWS[c]
                last = nc.tensor.transpose(ps[0:NE, 5, cols(c)], gate[0:n, c, 0:NE], ident[0:n, 0:n])
            last.then_inc(sem("gateT_ps"), 1)

            def combine():
                for half in range(2):
                    nc.tensor.matmul(ps[NS * half:NS * half + NS, 5, :], GT[:, cols(2)], ysb[:, 512 * half:512 * half + 512], start=True, stop=True)
                for c, bank in ((1, 3), (0, 6)):
                    for half in range(2):
                        last = nc.tensor.matmul(ps[:, bank + half, :], GT[:, cols(c)], ysb[:, 512 * half:512 * half + 512], start=True, stop=True)
                last.then_inc(sem("comb_ps"), 1)

            def gather(u, ks):
                for k in ks:
                    for c in range(3):
                        n = ROWS[c]
                        last = nc.tensor.matmul(ps[:, 5 * u, k * C:(k + 1) * C], xn[0:n, c, k * P:(k + 1) * P], S1[0:n, c, C * u:C * u + C], start=(c == 0), stop=(c == 2))
                if ks[-1] == KT - 1:
                    last.then_inc(sem("gather_ps"), 1)

            pe.wait_ge(sem("b2_in"), 16)
            pe.wait_ge(sem("moe_free"), 1)
            pe.wait_ge(sem("passes_ready"), 1)
            npass = pe.value_load(passes_i, min_val=1, max_val=MAX_PASS)
            with pe.Fori(0, npass) as p:
                pe.wait_ge(sem("S_ready"), p * (4 * PAIRS + 4) + 4)
                pe.wait_ge(sem("xT_ready"), p * (NE + 1) + 1)
                gather(0, range(KT))
                with pe.Fori(0, PAIRS) as pair:
                    pt = p * PAIRS + pair
                    for u in range(2):
                        et = 2 * pt + u
                        if u == 0:
                            pe.wait_ge(sem("sel_ready"), p * (PAIRS + 1) + pair + 1)
                        pe.wait_ge(sem("hid_read"), et + 1)
                        for m in range(2):
                            for half in range(2):
                                last = nc.tensor.matmul(ps[C * half:C * half + C, 1 + m, :], sel[0:96, u], b1p[0:96, D * half + 512 * m:D * half + 512 * m + 512], start=True, stop=False)
                        pe.wait_ge(sem("xT_ready"), p * (NE + 1) + 2 * pair + (2 + u))
                        for k in range(KT):
                            s = moe_slot(k)
                            pe.wait_ge(sem(f"slot_full{s}"), 32 * pt + (16 * u + moe_base(s) + 16))
                            for m in range(2):
                                for half in range(2):
                                    last = nc.tensor.matmul(ps[C * half:C * half + C, 1 + m, :], xT[:, k * C:(k + 1) * C],
                                                            slot(s)[:, D * half + 512 * m:D * half + 512 * m + 512], start=False, stop=(k == KT - 1))
                            last.then_inc(sem("expert_slot_used"), 1)
                        if u == 0:
                            pe.wait_ge(sem("GT_ready"), pt + 1)
                            pe.wait_ge(sem("ysb_ready"), 4 * pt + 1)
                            pe.wait_ge(sem("comb_read"), 4 * pt + 4)
                            combine()
                        else:
                            pe.wait_ge(sem("S_ready"), p * (4 * PAIRS + 4) + 4 * pair + 8)
                            gather(0, range(5))
                        pe.wait_ge(sem("g_ready"), et + 1)
                        for j in range(4):
                            last = nc.tensor.transpose(ps[:, 5 * u, j * P:(j + 1) * P], gg[:, j * P:(j + 1) * P], ident)
                        last.then_inc(sem("gT_ps"), 1)
                        if u == 0:
                            pe.wait_ge(sem("comb_read"), 4 * pt + 6)
                            gather(1, range(KT))
                            pe.wait_ge(sem("comb_read"), 4 * pt + 7)
                            for c in range(3):
                                n = ROWS[c]
                                last = nc.tensor.transpose(ps[:, 3, cols(c)], S2[0:n, c, :], ident[0:n, 0:n])
                            last.then_inc(sem("GT_ps"), 1)
                        else:
                            gather(0, range(5, KT))
                            pe.wait_ge(sem("ysb_ready"), 4 * pt + 3)
                        pe.wait_ge(sem("gT_ready"), et + 1)
                        for k in range(KT):
                            s = moe_slot(KT + k // 2)
                            if k % 2 == 0:
                                pe.wait_ge(sem(f"slot_full{s}"), 32 * pt + (16 * u + moe_base(s) + 16))
                            for half in range(2):
                                last = nc.tensor.matmul(ps[C * half:C * half + C, 4, :], gT[:, (k % 4) * P + C * (k // 4):(k % 4) * P + C * (k // 4) + C],
                                                        slot(s)[:, D * (k % 2) + 512 * half:D * (k % 2) + 512 * half + 512], start=(k == 0), stop=(k == KT - 1))
                            if k % 2 == 1:
                                last.then_inc(sem("expert_slot_used"), 1)
            pe.wait_ge(sem("GT_ready"), npass * PAIRS + 1)
            pe.wait_ge(sem("ysb_ready"), npass * (4 * PAIRS) + 1)
            pe.wait_ge(sem("comb_read"), npass * (4 * PAIRS) + 4)
            combine()


INPUTS = ["x_prompt", "x_sample", "state_conv", "state_ssm", "cache_win_k", "cache_win_v", "norm_mix", "w_in", "conv_w", "conv_b",
          "dt_bias", "a_log", "d_skip", "ssd_norm", "att_norm", "w_out", "norm_ffn", "router_w", "router_b", "w1", "b1", "w2", "b2", "norm_final"]
OUTPUTS = [("y_prompt", (SEQ, D), (1, SEQ, D)), ("y_sample", (NS, D), (DB, DT, D)),
           ("conv_prompt", (3, CD), (1, 1, 3, CD)), ("ssm_prompt", (H, HP, N), (1, 1, H, HP, N)),
           ("k_prompt", (SEQ, AH, AE), (1, 1, SEQ, AH, AE)), ("v_prompt", (SEQ, AH, AE), (1, 1, SEQ, AH, AE)),
           ("conv_sample", (DB, 3, CD), (1, DB, 3, CD)), ("ssm_sample", (DB, H, HP, N), (1, DB, H, HP, N)),
           ("k_sample", (NS, AH, AE), (1, DB, DT, AH, AE)), ("v_sample", (NS, AH, AE), (1, DB, DT, AH, AE))]


def kernel(**inputs):
    from concourse import bacc
    from concourse.bass_utils import run_bass_kernel_spmd

    nc = bacc.Bacc("TRN2", target_bir_lowering=False, num_devices=1)
    arrays = {name: np.ascontiguousarray(inputs[name]) for name in INPUTS}
    arrays |= {"consts": CONSTS, "bias_old": BIAS_OLD, "bias_prompt": BIAS_PROMPT}
    a = {n: nc.dram_tensor("in_" + n, v.shape, mybir.dt.from_np(v.dtype), kind="ExternalInput").ap() for n, v in arrays.items()}
    o = {n: nc.dram_tensor("out_" + n, shape, F32, kind="ExternalOutput").ap() for n, shape, _ in OUTPUTS}
    hymba_step(nc, a, o)
    r = run_bass_kernel_spmd(nc, [{"in_" + n: v for n, v in arrays.items()}], core_ids=[0])
    return tuple(r.results[0]["out_" + n].reshape(full) for n, _, full in OUTPUTS)
```
